# Optimizing a Trainium2 kernel written in Bass

```python
import math
import jax, jax.numpy as jnp
from jax import lax
import numpy as np

'''Two trunk layers of a hybrid diffusion / flow-matching backbone, run for two request groups that share weights.

Group (i), context pass: x_prompt (BATCH, SEQ, D_MODEL) context tokens, modulated by c_ctx (D_MODEL,); they read only context tokens.
Group (ii), denoising step: x_sample (DEC_BATCH, DEC_SEQ, D_MODEL) latent tokens on a GRID_W-wide grid, modulated by
c (DEC_BATCH, D_MODEL); they read all latent tokens plus PAST_LEN cached context tokens of each even layer:
  cache_diff_k  (DEC_BATCH, N_EVEN, PAST_LEN, H_DIFF, 2*DIFF_QK)  context keys of differential attention (two sub-keys, no position)
  cache_diff_v  (DEC_BATCH, N_EVEN, PAST_LEN, H_DIFF, DIFF_V)     context values of differential attention
  state_ret_fwd (DEC_BATCH, N_EVEN, H_RET, RET_DK, RET_DV)        final forward context retention state
  state_ret_bwd (DEC_BATCH, N_EVEN, H_RET, RET_DK, RET_DV)        final backward context retention state

Layer pattern: even layers = retention (A) + differential attention (B) as parallel head groups; odd layers = bidirectional
Hyena order-2 long convolution (C); each layer is followed by a group-limited top-2 MoE whose router is shared by all layers.
Post-LayerNorm with DeepNorm residual scaling; adaLN shift/scale/gate on both sub-layers.

Returns (y_prompt, y_sample, new_diff_k, new_diff_v, new_ret_state_fwd, new_ret_state_bwd):
  y_prompt          (BATCH, SEQ, D_MODEL)
  y_sample          (DEC_BATCH, DEC_SEQ, D_MODEL)
  new_diff_k        (BATCH, N_EVEN, SEQ, H_DIFF, 2*DIFF_QK)
  new_diff_v        (BATCH, N_EVEN, SEQ, H_DIFF, DIFF_V)
  new_ret_state_fwd (BATCH, N_EVEN, H_RET, RET_DK, RET_DV)
  new_ret_state_bwd (BATCH, N_EVEN, H_RET, RET_DK, RET_DV)
'''

D_MODEL = 1024
BATCH = 1
SEQ = 128
DEPTH = 2
DEC_BATCH = 1
DEC_SEQ = 256
PAST_LEN = 128

GRID_W = 64
N_EVEN = (DEPTH + 1) // 2
N_ODD = DEPTH // 2
H_RET = 4
RET_DK = 128
RET_DV = 128
RET_W = H_RET * RET_DV
RET_CHUNK = 128
H_DIFF = 4
DIFF_QK = 64
DIFF_V = 128
DIFF_W = H_DIFF * DIFF_V
Q_BLOCK = 128
ROPE_BASE = 10000.0
HY_BANDS = 16
HY_EMB = 1 + 2 * HY_BANDS
HY_FH = 64
HY_DECAY_TARGET = 1e-2
HY_FAST = 0.3
HY_SLOW = 1.5
HY_SHIFT = 0.05
N_EXPERTS = 16
N_GROUPS = 4
TOP_K = 2
D_FF_EXPERT = 512
ALPHA = (2 * DEPTH) ** 0.25
BETA = (8 * DEPTH) ** -0.25
LN_EPS = 1e-5

kernel_name = 'hybrid_retention_diffattn_hyena_moe_diffusion_step'

def layer_norm(x, w, b):
    xf = x.astype(jnp.float32)
    mu = xf.mean(-1, keepdims=True)
    var = jnp.square(xf - mu).mean(-1, keepdims=True)
    y = (xf - mu) * lax.rsqrt(var + LN_EPS) * w.astype(jnp.float32) + b.astype(jnp.float32)
    return y.astype(x.dtype)

def axial_rope(x):
    L = x.shape[1]
    d = x.shape[-1]
    half = d // 2
    quarter = half // 2
    rows = L // GRID_W
    t = jnp.arange(rows * GRID_W)
    row = (t // GRID_W).astype(jnp.float32)
    col = (t % GRID_W).astype(jnp.float32)
    inv = ROPE_BASE ** (-jnp.arange(quarter, dtype=jnp.float32) / quarter)
    bshape = (L,) + (1,) * (x.ndim - 3) + (quarter,)

    def rot(xh, pos):
        ang = (pos[:, None] * inv[None, :]).reshape(bshape)
        cos, sin = jnp.cos(ang), jnp.sin(ang)
        x1, x2 = xh[..., :quarter], xh[..., quarter:]
        return jnp.concatenate([x1 * cos - x2 * sin, x1 * sin + x2 * cos], axis=-1)

    xf = x.astype(jnp.float32)
    return jnp.concatenate([rot(xf[..., :half], row), rot(xf[..., half:], col)], axis=-1).astype(x.dtype)

def retention_dir(q, k, v, log_gamma, s0):
    B, L, H, dk = q.shape
    dv = v.shape[-1]
    n = L // RET_CHUNK
    qc = q.reshape(B, n, RET_CHUNK, H, dk)
    kc = k.reshape(B, n, RET_CHUNK, H, dk)
    vc = v.reshape(B, n, RET_CHUNK, H, dv)
    idx = jnp.arange(RET_CHUNK, dtype=jnp.float32)
    rel = idx[:, None] - idx[None, :]
    dmat = jnp.where(rel >= 0, jnp.exp(jnp.maximum(rel, 0.0)[None] * log_gamma[:, None, None]), 0.0)
    xi = jnp.exp((idx + 1.0)[None, :] * log_gamma[:, None])
    zeta = jnp.exp((RET_CHUNK - 1.0 - idx)[None, :] * log_gamma[:, None])
    g_chunk = jnp.exp(RET_CHUNK * log_gamma)
    scores = jnp.einsum('bnihd,bnjhd->bnhij', qc, kc) * dmat
    inner = jnp.einsum('bnhij,bnjhe->bnihe', scores, vc)
    kv = jnp.einsum('bnjhd,hj,bnjhe->nbhde', kc, zeta, vc)

    def step(s, kv_i):
        return g_chunk[:, None, None] * s + kv_i, s

    s_final, s_prev = lax.scan(step, s0, kv)
    cross = jnp.einsum('bnihd,nbhde,hi->bnihe', qc, s_prev, xi)
    return (inner + cross).reshape(B, L, H, dv), s_final

def diff_attention(q, k, v, lam):
    B, Lq, H, _, dq = q.shape
    nb = Lq // Q_BLOCK
    qb = jnp.moveaxis(q.reshape(B, nb, Q_BLOCK, H, 2, dq), 1, 0)
    scale = dq ** -0.5
    vf = v.astype(jnp.float32)

    def block(qi):
        s = jnp.einsum('bqhrd,bkhrd->bhrqk', qi, k).astype(jnp.float32) * scale
        p = jax.nn.softmax(s, axis=-1)
        a = p[:, :, 0] - lam * p[:, :, 1]
        return jnp.einsum('bhqk,bkhd->bqhd', a, vf)

    o = lax.map(block, qb)
    return jnp.moveaxis(o, 0, 1).reshape(B, Lq, H, v.shape[-1])

def implicit_filter(L, w1, b1, w2, b2, w3, freq):
    f32 = jnp.float32
    t = jnp.linspace(0.0, 1.0, L, dtype=f32)[:, None]
    bands = jnp.linspace(1e-4, HY_BANDS - 1, HY_BANDS, dtype=f32)
    ang = 2.0 * math.pi * bands[None, :] * jnp.arange(L, dtype=f32)[:, None] / L
    z = jnp.concatenate([t, jnp.cos(ang), -jnp.sin(ang)], axis=-1)
    fr = freq.astype(f32)
    a = jnp.sin(fr * (z @ w1.astype(f32) + b1.astype(f32)))
    a = jnp.sin(fr * (a @ w2.astype(f32) + b2.astype(f32)))
    filt = a @ w3.astype(f32)
    deltas = jnp.abs(jnp.linspace(math.log(HY_DECAY_TARGET) / HY_SLOW,
                                  math.log(HY_DECAY_TARGET) / HY_FAST, D_MODEL, dtype=f32))
    window = jnp.exp(-t * deltas[None, :]) + HY_SHIFT
    return filt[:, :D_MODEL] * window, filt[:, D_MODEL:] * window

def bidir_fft_conv(u, h_fwd, h_bwd, bias):
    L = u.shape[1]
    D = u.shape[2]
    uf = u.astype(jnp.float32)
    taps = jnp.concatenate([h_fwd, jnp.zeros((1, D), jnp.float32), h_bwd[1:][::-1]], axis=0)
    spec = jnp.fft.rfft(uf, n=2 * L, axis=1) * jnp.fft.rfft(taps, n=2 * L, axis=0)[None]
    y = jnp.fft.irfft(spec, n=2 * L, axis=1)[:, :L]
    return (y + uf * bias.astype(jnp.float32)).astype(u.dtype)

def moe_ffn(h, router_w, router_bias, w_gate, w_up, w_down):
    B, L, D = h.shape
    t = h.reshape(B * L, D)
    T = t.shape[0]
    scores = jax.nn.sigmoid((t @ router_w).astype(jnp.float32))
    sel = scores + router_bias.astype(jnp.float32)
    grp = sel.reshape(T, N_GROUPS, N_EXPERTS // N_GROUPS)
    gscore = lax.top_k(grp, TOP_K)[0].sum(-1)
    gmask = jax.nn.one_hot(jnp.argmax(gscore, axis=-1), N_GROUPS) > 0
    emask = jnp.repeat(gmask, N_EXPERTS // N_GROUPS, axis=-1)
    _, eidx = lax.top_k(jnp.where(emask, sel, -jnp.inf), TOP_K)
    wsel = jnp.take_along_axis(scores, eidx, axis=-1)
    wsel = wsel / wsel.sum(-1, keepdims=True)
    comb = jnp.sum(jax.nn.one_hot(eidx, N_EXPERTS, dtype=jnp.float32) * wsel[..., None], axis=1)
    hg = jnp.einsum('td,edf->tef', t, w_gate)
    hu = jnp.einsum('td,edf->tef', t, w_up)
    act = jax.nn.silu(hg) * hu * comb[:, :, None].astype(t.dtype)
    return jnp.einsum('tef,efd->td', act, w_down).reshape(B, L, D)

def even_mixer(h, P, e, l, ctx):
    B, L, _ = h.shape
    f32 = jnp.float32
    proj = h @ P['ev_w_in'][e]
    widths = [H_RET * RET_DK, H_RET * RET_DK, RET_W, RET_W, H_DIFF * 2 * DIFF_QK, H_DIFF * 2 * DIFF_QK, DIFF_W]
    q_r, k_r, v_r, g_r, q_d, k_d, v_d = jnp.split(proj, np.cumsum(widths)[:-1].tolist(), axis=-1)
    q_r = q_r.reshape(B, L, H_RET, RET_DK)
    k_r = k_r.reshape(B, L, H_RET, RET_DK) * (RET_DK ** -0.5)
    v_r = v_r.reshape(B, L, H_RET, RET_DV)
    q_d = q_d.reshape(B, L, H_DIFF, 2, DIFF_QK)
    k_d = k_d.reshape(B, L, H_DIFF, 2, DIFF_QK)
    v_d = v_d.reshape(B, L, H_DIFF, DIFF_V)
    k_d_ctx = k_d.reshape(B, L, H_DIFF, 2 * DIFF_QK)
    if ctx is None:
        s0f = jnp.zeros((B, H_RET, RET_DK, RET_DV), f32)
        s0b = s0f
        k_all, v_all = k_d, v_d
    else:
        ck, cv, s0f, s0b = ctx
        q_r, k_r = axial_rope(q_r), axial_rope(k_r)
        q_d, k_d = axial_rope(q_d), axial_rope(k_d)
        k_all = jnp.concatenate([k_d, ck.reshape(B, -1, H_DIFF, 2, DIFF_QK).astype(k_d.dtype)], axis=1)
        v_all = jnp.concatenate([v_d, cv.astype(v_d.dtype)], axis=1)
    lgf = jnp.log1p(-jnp.exp2(P['ret_decay_fwd'][e].astype(f32)))
    lgb = jnp.log1p(-jnp.exp2(P['ret_decay_bwd'][e].astype(f32)))
    qf, kf, vf = q_r.astype(f32), k_r.astype(f32), v_r.astype(f32)
    of, sf = retention_dir(qf, kf, vf, lgf, s0f.astype(f32))
    ob, sb = retention_dir(qf[:, ::-1], kf[:, ::-1], vf[:, ::-1], lgb, s0b.astype(f32))
    ret = of + ob[:, ::-1]
    mu = ret.mean(-1, keepdims=True)
    var = jnp.square(ret - mu).mean(-1, keepdims=True)
    ret = ((ret - mu) * lax.rsqrt(var + LN_EPS)).reshape(B, L, RET_W) * P['ret_gn_w'][e].astype(f32)
    ret = jax.nn.silu(g_r.astype(f32)) * ret
    lam_init = 0.8 - 0.6 * math.exp(-0.3 * l)
    lq1, lk1, lq2, lk2 = P['diff_lambda'][e].astype(f32)
    lam = jnp.exp(jnp.sum(lq1 * lk1)) - jnp.exp(jnp.sum(lq2 * lk2)) + lam_init
    att = diff_attention(q_d, k_all, v_all, lam)
    att = att * lax.rsqrt(jnp.mean(jnp.square(att), -1, keepdims=True) + LN_EPS)
    att = (att * P['diff_subln_w'][e].astype(f32) * (1.0 - lam_init)).reshape(B, L, DIFF_W)
    out = jnp.concatenate([ret, att], axis=-1).astype(h.dtype) @ P['ev_w_out'][e]
    return out, (k_d_ctx, v_d, sf.astype(h.dtype), sb.astype(h.dtype))

def hyena_mixer(h, P, o):
    B, L, D = h.shape
    u = h @ P['hy_w_in'][o]
    cw = P['hy_conv_w'][o]
    up = jnp.pad(u, ((0, 0), (1, 1), (0, 0)))
    u = up[:, :-2] * cw[0] + up[:, 1:-1] * cw[1] + up[:, 2:] * cw[2] + P['hy_conv_b'][o]
    x0, x1, v = jnp.split(u, 3, axis=-1)
    hf, hb = implicit_filter(L, P['hy_ffn_w1'][o], P['hy_ffn_b1'][o], P['hy_ffn_w2'][o],
                             P['hy_ffn_b2'][o], P['hy_ffn_w3'][o], P['hy_freq'][o])
    z = bidir_fft_conv(x1 * v, hf, hb, P['hy_filter_bias'][o])
    return (x0 * z) @ P['hy_w_out'][o]

def trunk(x, cond, P, caches):
    produced = []
    for l in range(DEPTH):
        mod = jax.nn.silu(cond) @ P['ada_w'][l] + P['ada_b'][l]
        sh1, sc1, g1, sh2, sc2, g2 = jnp.split(mod[:, None, :], 6, axis=-1)
        h = x * (1.0 + sc1) + sh1
        if l % 2 == 0:
            e = l // 2
            ctx = None if caches is None else caches[e]
            out, ctx_new = even_mixer(h, P, e, l, ctx)
            if caches is None:
                produced.append(ctx_new)
        else:
            out = hyena_mixer(h, P, l // 2)
        x = layer_norm(ALPHA * x + g1 * out, P['ln_w'][l, 0], P['ln_b'][l, 0])
        h = x * (1.0 + sc2) + sh2
        y = moe_ffn(h, P['router_w'], P['router_bias'], P['moe_w_gate'][l], P['moe_w_up'][l], P['moe_w_down'][l])
        x = layer_norm(ALPHA * x + g2 * y, P['ln_w'][l, 1], P['ln_b'][l, 1])
    return x, produced

def setup_inputs(seed: int = 0) -> dict:
    key = jax.random.key(seed)
    ks = jax.random.split(key, 36)
    f32 = jnp.float32
    D = D_MODEL

    def nrm(k, shape, s):
        return jax.random.normal(k, shape, f32) * s

    ev_in = 2 * H_RET * RET_DK + 2 * RET_W + 2 * H_DIFF * 2 * DIFF_QK + DIFF_W
    decay_base = -(5.0 + jnp.arange(H_RET, dtype=f32))[None, :]
    return {
        'x_prompt': nrm(ks[0], (BATCH, SEQ, D), 1.0),
        'x_sample': nrm(ks[1], (DEC_BATCH, DEC_SEQ, D), 1.0),
        'cache_diff_k': nrm(ks[2], (DEC_BATCH, N_EVEN, PAST_LEN, H_DIFF, 2 * DIFF_QK), 1.0),
        'cache_diff_v': nrm(ks[3], (DEC_BATCH, N_EVEN, PAST_LEN, H_DIFF, DIFF_V), 1.0),
        'state_ret_fwd': nrm(ks[4], (DEC_BATCH, N_EVEN, H_RET, RET_DK, RET_DV), 0.3),
        'state_ret_bwd': nrm(ks[5], (DEC_BATCH, N_EVEN, H_RET, RET_DK, RET_DV), 0.3),
        'c': nrm(ks[6], (DEC_BATCH, D), 1.0),
        'c_ctx': nrm(ks[7], (D,), 1.0),
        'ada_w': nrm(ks[8], (DEPTH, D, 6 * D), D ** -0.5),
        'ada_b': nrm(ks[9], (DEPTH, 6 * D), 0.01),
        'ln_w': 1.0 + nrm(ks[10], (DEPTH, 2, D), 0.01),
        'ln_b': nrm(ks[11], (DEPTH, 2, D), 0.01),
        'ev_w_in': nrm(ks[12], (N_EVEN, D, ev_in), D ** -0.5),
        'ev_w_out': nrm(ks[13], (N_EVEN, RET_W + DIFF_W, D), BETA * (RET_W + DIFF_W) ** -0.5),
        'ret_decay_fwd': decay_base + nrm(ks[14], (N_EVEN, H_RET), 0.1),
        'ret_decay_bwd': decay_base + nrm(ks[15], (N_EVEN, H_RET), 0.1),
        'ret_gn_w': 1.0 + nrm(ks[16], (N_EVEN, RET_W), 0.01),
        'diff_lambda': nrm(ks[17], (N_EVEN, 4, DIFF_QK), 0.1),
        'diff_subln_w': 1.0 + nrm(ks[18], (N_EVEN, DIFF_V), 0.01),
        'hy_w_in': nrm(ks[19], (N_ODD, D, 3 * D), D ** -0.5),
        'hy_conv_w': nrm(ks[20], (N_ODD, 3, 3 * D), 3 ** -0.5),
        'hy_conv_b': nrm(ks[21], (N_ODD, 3 * D), 0.01),
        'hy_ffn_w1': nrm(ks[22], (N_ODD, HY_EMB, HY_FH), HY_EMB ** -0.5),
        'hy_ffn_b1': nrm(ks[23], (N_ODD, HY_FH), 0.01),
        'hy_ffn_w2': nrm(ks[24], (N_ODD, HY_FH, HY_FH), HY_FH ** -0.5),
        'hy_ffn_b2': nrm(ks[25], (N_ODD, HY_FH), 0.01),
        'hy_ffn_w3': nrm(ks[26], (N_ODD, HY_FH, 2 * D), 0.1 * HY_FH ** -0.5),
        'hy_freq': 1.0 + nrm(ks[27], (N_ODD, HY_FH), 0.01),
        'hy_filter_bias': nrm(ks[28], (N_ODD, D), 0.5),
        'hy_w_out': nrm(ks[29], (N_ODD, D, D), BETA * D ** -0.5),
        'router_w': nrm(ks[30], (D, N_EXPERTS), D ** -0.5),
        'router_bias': nrm(ks[31], (N_EXPERTS,), 0.01),
        'moe_w_gate': nrm(ks[32], (DEPTH, N_EXPERTS, D, D_FF_EXPERT), D ** -0.5),
        'moe_w_up': nrm(ks[33], (DEPTH, N_EXPERTS, D, D_FF_EXPERT), D ** -0.5),
        'moe_w_down': nrm(ks[34], (DEPTH, N_EXPERTS, D_FF_EXPERT, D), BETA * D_FF_EXPERT ** -0.5),
    }

def reference(x_prompt, x_sample, cache_diff_k, cache_diff_v, state_ret_fwd, state_ret_bwd, c, c_ctx,
              ada_w, ada_b, ln_w, ln_b, ev_w_in, ev_w_out, ret_decay_fwd, ret_decay_bwd, ret_gn_w,
              diff_lambda, diff_subln_w, hy_w_in, hy_conv_w, hy_conv_b, hy_ffn_w1, hy_ffn_b1, hy_ffn_w2,
              hy_ffn_b2, hy_ffn_w3, hy_freq, hy_filter_bias, hy_w_out, router_w, router_bias,
              moe_w_gate, moe_w_up, moe_w_down):
    P = {
        'ada_w': ada_w, 'ada_b': ada_b, 'ln_w': ln_w, 'ln_b': ln_b,
        'ev_w_in': ev_w_in, 'ev_w_out': ev_w_out, 'ret_decay_fwd': ret_decay_fwd,
        'ret_decay_bwd': ret_decay_bwd, 'ret_gn_w': ret_gn_w, 'diff_lambda': diff_lambda,
        'diff_subln_w': diff_subln_w, 'hy_w_in': hy_w_in, 'hy_conv_w': hy_conv_w, 'hy_conv_b': hy_conv_b,
        'hy_ffn_w1': hy_ffn_w1, 'hy_ffn_b1': hy_ffn_b1, 'hy_ffn_w2': hy_ffn_w2, 'hy_ffn_b2': hy_ffn_b2,
        'hy_ffn_w3': hy_ffn_w3, 'hy_freq': hy_freq, 'hy_filter_bias': hy_filter_bias, 'hy_w_out': hy_w_out,
        'router_w': router_w, 'router_bias': router_bias,
        'moe_w_gate': moe_w_gate, 'moe_w_up': moe_w_up, 'moe_w_down': moe_w_down,
    }
    y_prompt, produced = trunk(x_prompt, c_ctx[None, :], P, None)
    new_diff_k = jnp.stack([p[0] for p in produced], axis=1)
    new_diff_v = jnp.stack([p[1] for p in produced], axis=1)
    new_ret_state_fwd = jnp.stack([p[2] for p in produced], axis=1)
    new_ret_state_bwd = jnp.stack([p[3] for p in produced], axis=1)
    caches = [(cache_diff_k[:, e], cache_diff_v[:, e], state_ret_fwd[:, e], state_ret_bwd[:, e])
              for e in range(N_EVEN)]
    y_sample, _ = trunk(x_sample, c, P, caches)
    return (y_prompt, y_sample, new_diff_k, new_diff_v, new_ret_state_fwd, new_ret_state_bwd)


_drawn_inputs = setup_inputs


def setup_inputs(seed=0):
    import zlib

    import numpy as np

    out = dict(_drawn_inputs(seed))
    spreads = {}
    factors = {'state_ret_fwd': 2.84,
     'state_ret_bwd': 2.918,
     'ret_gn_w': 20.694,
     'diff_lambda': 2.819,
     'diff_subln_w': 23.337,
     'hy_conv_b': 9.774,
     'hy_ffn_b1': 8.0,
     'hy_ffn_b2': 4.318,
     'hy_freq': 8.0}
    for name, (base, spread) in spreads.items():
        noise = np.random.default_rng([zlib.crc32(name.encode()), seed]).standard_normal(out[name].shape)
        drawn = base * np.exp(spread * noise) if base else spread * noise
        out[name] = __import__('jax').numpy.asarray(drawn.astype(out[name].dtype))
    for name, factor in factors.items():
        out[name] = (out[name] * factor).astype(out[name].dtype)
    return out
```

```python
import math
from contextlib import ExitStack

import concourse.bass as bass
from concourse import mybir
import numpy as np

F32 = mybir.dt.float32
I32 = mybir.dt.int32
ACT = mybir.ActivationFunctionType
ALU = mybir.AluOpType
AX = mybir.AxisListType.X

P = 128
D = 1024
KT = D // P
NT = 3
T = NT * P
CTX = P
H = 4
EV_CHUNKS = 7
NE = 16
NG = 4
FT = 4
BLK = 128
MAX_BLOCKS = NE + 2 * T // BLK
HY_T = 24
FH = 64
EMB = 33
ALPHA = 4 ** 0.25
EPS = 1e-5
LAM_INIT = 0.8 - 0.6 * math.exp(0.0)
QK_SCALE = 64 ** -0.5
BIG = 1e30
ROUND = 1.5 * 2.0 ** 23
TWO_PI_HI = 6.28125
TWO_PI_LO = 2 * math.pi - 6.28125
RING = 6
CHUNK = 4096

ADA0, EVIN = 0, 12
EVOUT = EVIN + EV_CHUNKS
MOE0 = EVOUT + 2
ADA1 = MOE0 + 3 * NE
HYIN = ADA1 + 12
HYOUT = HYIN + 6
MOE1 = HYOUT + 2
CHUNKS = MOE1 + 3 * NE

K_ID, K_TRI, K_ONE, K_KEYG, K_KEYE, K_WF, K_LEFT, K_J = 0, 128, 256, 384, 388, 404, 407, 408
K_N = 409
M_RELF, M_RELB, M_MF, M_MB, M_XI, M_XB, M_RC, M_RS, M_DC, M_DS = (
    0, 128, 256, 384, 512, 640, 768, 1024, 1280, 1408)
M_N = 1536
DFT_N = 1280


def constants():
    i = np.arange(P)
    keep = np.zeros((P, K_N))
    keep[:, K_ID:K_ID + P] = np.eye(P)
    keep[:, K_TRI:K_TRI + P] = i[:, None] < i[None, :]
    keep[:, K_ONE:K_ONE + P] = 1
    keep[:, K_KEYG:K_KEYG + NG] = NG - np.arange(NG)
    keep[:, K_KEYE:K_KEYE + NE] = NE - np.arange(NE)
    n_ctx, n_smp = 2 * CTX - 1, 2 * (T - CTX) - 1
    keep[:, K_WF] = np.where(i == 0, 1, 2) / n_ctx
    keep[:, K_WF + 1] = np.where(i == 0, 1, 2) / n_smp
    keep[:, K_WF + 2] = 2 / n_smp
    keep[:, K_LEFT] = P - 1 - i
    keep[:, K_J] = i

    mix = np.zeros((P, M_N))
    rel = i[None, :] - i[:, None]
    scale = P ** -0.5
    mix[:, M_RELF:M_RELF + P] = np.maximum(rel, 0)
    mix[:, M_RELB:M_RELB + P] = np.maximum(-rel, 0)
    mix[:, M_MF:M_MF + P] = (rel >= 0) * scale
    mix[:, M_MB:M_MB + P] = (rel <= 0) * scale
    mix[:, M_XI:M_XI + P] = i[None, :] + 1
    mix[:, M_XB:M_XB + P] = P - i[None, :]
    for tile in range(2):
        t = np.arange(tile * P, tile * P + P)
        for width, c0, s0 in ((128, M_RC, M_RS), (64, M_DC, M_DS)):
            quarter = width // 4
            inv = (10000.0 ** (-np.arange(quarter, dtype=np.float32) / quarter)).astype(np.float32)
            for a, pos in enumerate((t // 64, t % 64)):
                ang = (pos[:, None].astype(np.float32) * inv[None, :]).astype(np.float64)
                for two in range(2):
                    at = tile * width + (2 * a + two) * quarter
                    mix[:, c0 + at:c0 + at + quarter] = np.cos(ang)
                    mix[:, s0 + at:s0 + at + quarter] = np.sin(ang) * (1 if two else -1)

    dft = np.zeros((P, DFT_N))
    for n, base, tiles in ((n_ctx, 0, 1), (n_smp, 256, 2)):
        for k, trig in enumerate((np.cos, np.sin)):
            for tile in range(tiles):
                width = tiles * P
                at = base + (k * tiles + tile) * width
                t = np.arange(tile * P, tile * P + P)
                dft[:, at:at + width] = trig(2 * np.pi * ((t[:, None] * np.arange(width)[None, :]) % n) / n)

    feats, wins = [], []
    for L in (CTX, T - CTX):
        t = np.linspace(0.0, 1.0, L, dtype=np.float32)[:, None].astype(np.float64)
        bands = np.linspace(1e-4, 15, 16, dtype=np.float32).astype(np.float64)
        ang = 2.0 * math.pi * bands[None, :] * np.arange(L)[:, None] / L
        feats.append(np.concatenate([t, np.cos(ang), -np.sin(ang)], axis=-1).T)
        deltas = np.abs(np.linspace(math.log(1e-2) / 1.5, math.log(1e-2) / 0.3, D, dtype=np.float32)).astype(np.float64)
        wins.append(np.exp(-t * deltas[None, :]) + 0.05)
    feats = np.concatenate(feats, axis=1)
    win = np.concatenate(wins, axis=0)
    return {k: np.ascontiguousarray(v, dtype=np.float32) for k, v in
            dict(c_keep=keep, c_mix=mix, c_dft=dft, c_feat=feats, c_win=win).items()}


def trunk_program(nc, a, out):
    ctx = ExitStack()
    with ctx:
        def sb(name, shape, dt=F32):
            return ctx.enter_context(nc.sbuf_tensor(name, shape, dt))

        def sem(name):
            return ctx.enter_context(nc.semaphore(name))

        ring = sb("ring", [P, RING, CHUNK])
        x = sb("x", [P, NT, D])
        hT = sb("hT", [P, KT, T])
        arena = sb("arena", [P, 19456])
        keep = sb("keep", [P, K_N])
        small = sb("small", [P, 1600])
        idx = sb("idx", [P, 2 * NT], I32)
        table = sb("table", [1, NE + 1], I32)
        bank = [ctx.enter_context(nc.psum_tensor(f"bank{i}", [P, 512], F32))[:, :] for i in range(8)]
        slots = nc.dram_tensor("slot_rows", [(MAX_BLOCKS + 2) * BLK, D], F32).ap()

        gates = nc.dram_tensor("gate_rows", [2, 2, 2, D], F32).ap()

        def at(off, *dims, rows=P, src=arena):
            n = math.prod(dims)
            v = src[0:rows, off:off + n]
            if len(dims) == 2:
                return v.rearrange("p (a b) -> p a b", b=dims[1])
            if len(dims) == 3:
                return v.rearrange("p (a b c) -> p a b c", b=dims[1], c=dims[2])
            return v

        top = [0]

        def tiny(*dims, rows=P):
            off = top[0]
            top[0] += math.prod(dims)
            return at(off, *dims, rows=rows, src=small)

        ident = keep[:, K_ID:K_ID + P]
        tri = keep[:, K_TRI:K_TRI + P]
        ones = keep[:, K_ONE:K_ONE + P]
        xf = x[:, :, :].rearrange("p t d -> p (t d)")
        hf = hT[:, :, :].rearrange("p k t -> p (k t)")

        router_w = tiny(KT, NE)
        router_b = tiny(NE)
        condT = tiny(KT * 2)
        modT = tiny(48, 2)
        gn_w = tiny(512)
        lam_in = tiny(4, 64)
        subln = tiny(P)
        decay = tiny(2 * H)
        lg = tiny(2 * H)
        lgt = tiny(4, 2 * H)
        g_chunk = tiny(2 * H)
        zeta = tiny(2, H)
        lam = tiny(4)
        stats = tiny(NT, 12)
        mv = tiny(NT, 2)
        sd = tiny(NT)
        rstd = tiny(NT)
        nmr = tiny(NT)
        hy_cols = tiny(104)
        ffn_cols = tiny(3, rows=FH)

        ada_bias = at(0, 6 * D, rows=2)
        mod_rows = [at(6144, 6 * D, rows=2), ada_bias]
        cond_rows = at(18432, P, rows=16)
        hy_rows = at(18560, P, rows=104)
        proj = at(0, NT, EV_CHUNKS, 512)
        QR, KR, VR, GR, QD, KD, VD = range(EV_CHUNKS)
        mixc = at(12288, M_N)
        qdT = at(10752, H, T)
        kdT = at(12288, H, T)
        ckT = at(13824, H, P)
        cv = at(14336, H, P)
        decay_T = at(14848, H, P)
        xi_f = at(15360, H, P)
        xi_b = at(15872, H, P)
        s0 = at(16384, 2, H, P)
        s1 = at(17408, 2, H, P)
        s_out = at(18432, 2, H, P)
        zeros = at(18432, D, rows=BLK)
        decay_bwd = s1[:, 0]
        qrT = at(0, H, T, src=hf)
        krT = at(1536, H, T, src=hf)
        rope_tmp = at(0, 512, src=xf)
        qxi = at(0, 4, H, P, src=xf)
        kz23 = at(2048, 2, 512, src=xf)
        ck_raw = at(2560, 512, src=xf)
        probs = at(0, 2, 2, 384, src=xf)
        adiff = at(1536, 2, 384, src=xf)
        adT = at(2304, 2, 384, src=xf)
        h_tok = at(0, NT, D)
        slot_in = at(3072, D, rows=BLK)
        slot_inT = at(4096, KT, BLK)
        silu_g = at(5120, FT * BLK)
        act_T = at(5632, FT, BLK)
        yT = at(6144, KT, BLK)
        slot_out = at(7168, D, rows=BLK)
        picked = at(8192, NT, 2, D)
        x0T = at(0, KT, T)
        ufT = at(3072, KT, T)
        u_tok = at(6144, NT, 512)
        win = [at(7680, NT, 512), at(0, NT, 512, src=hf)]
        hsd = at(9216, 2, NT, 512)
        spec = at(12288, 2, NT, 512)
        prod = at(15360, 4, 512)
        w3 = [at(12288, 2, 512, rows=FH), at(1536, 2, 512, rows=FH, src=hf)]
        vT = at(15360, 2, T)
        dft = at(17408, DFT_N)
        feat = at(18688, T, rows=EMB)
        arg = at(16384, T, rows=FH)
        turns = at(16768, T, rows=FH)
        sinT = at(19072, T, rows=FH)
        w1 = at(9216, FH, rows=EMB)
        w2 = at(9344, FH, rows=FH)
        LN_AT = [(0, 4096), (14336, None), (6144, 10240), (14336, None)]

        R0 = 9000

        def rt(k, *dims):
            return at(R0 + 48 * k, *dims)
        score, sel, selm, eq, oh0, oh1, mask, soff = [rt(k, NT, NE) for k in range(8)]
        hi2, lo2 = rt(8, NT * NG, 2), rt(9, NT * NG, 2)
        m1, m2, gs, pen = [at(R0 + 480 + 12 * k, NT * NG) for k in range(4)]
        rmx = at(R0 + 528, NT)
        nblk = at(R0 + 540, 2, NE)
        base = at(R0 + 580, NE + 1)
        slot_f = at(R0 + 600, 2, NT)
        wsel = tiny(3, NT)
        mx = tiny(12, 2)
        nmx = tiny(12, 2)
        ssum = tiny(12, 2)
        rsum = tiny(12, 2)
        hstat = tiny(H, 6)
        hmv = tiny(NT, H, 2)
        hsd_ = tiny(NT, H)
        hrs = tiny(NT, H)
        eps_col = tiny(1)
        idle = tiny(1)
        assert top[0] <= 1600

        ring_full = [sem(f"ring_full{s}") for s in range(RING)]
        const_in, x_in, mix_in, hy_in_s, adab_in = [sem(n) for n in ("const_in", "x_in", "mix_in", "hy_in", "adab_in")]
        mixc_in, ck_in = sem("mixc_in"), sem("ck_in")
        act_chain, dve_chain = sem("act_chain"), sem("dve_chain")
        cond_act, condT_mm, condT_rdy = sem("cond_act"), sem("condT_mm"), sem("condT_ready")
        ada_mm, mod_row, modT_mm, modT_rdy = sem("ada_mm"), sem("mod_row"), sem("modT_mm"), sem("modT_ready")
        gate_out = sem("gate_out")
        xT_mm, hT_act, hT_dve = sem("xT_mm"), sem("hT_act"), sem("hT_dve")
        lg_rdy, tab_act, tab_dve = sem("lg_ready"), sem("tab_act"), sem("tab_dve")
        proj_mm, proj_act, proj_dve = sem("proj_mm"), sem("proj_act"), sem("proj_dve")
        qkT_mm, qkT_act, qkT_dve = sem("qkT_mm"), sem("qkT_act"), sem("qkT_dve")
        rsc_mm, rsc_dve, kz_dve, kv_mm, kv_act, kv_dve = [sem(n) for n in (
            "rsc_mm", "rsc_dve", "kz_dve", "kv_mm", "kv_act", "kv_dve")]
        ret_mm, ret_var, ret_sd, ret_dve = [sem(n) for n in ("ret_mm", "ret_var", "ret_sd", "ret_dve")]
        dsc_mm, dmax, dexp, dcomb, daT_mm, daT, dpv_mm = [sem(n) for n in (
            "dsc_mm", "dmax", "dexp", "dcomb", "daT_mm", "daT", "dpv_mm")]
        att_ss, att_sd, att_dve = sem("att_ss"), sem("att_sd"), sem("att_dve")
        cT_mm, cT_act, cT_dve = sem("cT_mm"), sem("cT_act"), sem("cT_dve")
        mix_mm = [sem("mix_mm0"), sem("mix_mm1")]
        ln_in, ln_var, ln_sd, ln_rstd, ln_nrm, ln_w, x_rdy = [sem(n) for n in (
            "ln_in", "ln_var", "ln_sd", "ln_rstd", "ln_nrm", "ln_w", "x_ready")]
        x_again = sem("x_again")
        rlog_mm, rscore, htok_mm, htok_act = [sem(n) for n in ("rlog_mm", "rscore", "htok_mm", "htok_act")]
        mask_rdy, pos_mm, table_rdy, idx_rdy, zero_rdy, zeroed, scattered, ln_first = [sem(n) for n in (
            "mask_ready", "pos_mm", "table_ready", "idx_ready", "zero_ready", "zeroed", "scattered", "rows_scaled")]
        MS = [{n: sem(f"{n}_{layer}") for n in (
            "row_in", "rowT_mm", "rowT", "gate_mm", "silu", "up_mm", "act", "down_mm", "downT", "back_mm",
            "slot_evac", "slot_stored")} for layer in range(2)]
        fmm, farg, fsin = sem("filter_mm"), sem("filter_arg"), sem("filter_sin")
        hyc_mm, hyc = sem("hycols_mm"), sem("hycols")
        hy_mm, hy_act, hy_dve = sem("hy_mm"), sem("hy_act"), sem("hy_dve")
        taps_in = [sem("taps_in0"), sem("taps_in1")]
        dft_in = sem("dft_in")
        tap_mm, tap_dve, sp_mm, sp_act, ut_mm, ut_act, us_mm, us_dve, inv_mm, inv_dve = [sem(n) for n in (
            "tap_mm", "tap_dve", "spec_mm", "spec_act", "ut_mm", "ut_act", "us_mm", "us_dve", "inv_mm", "inv_dve")]
        lnrow_in = sem("lnrow_in")
        gathered = [sem(f"gathered{t}") for t in range(NT)]
        out_done = sem("out_done")
        idle_set = sem("idle_set")
        router_in = sem("router_in")
        first_in = sem("first_in")
        x_out = sem("x_out")
        OUT_DMAS = 4

        def cols(w, c):
            return w[:, c * 512:(c + 1) * 512].rearrange("(k p) n -> p k n", p=P)

        def chunk_src(n):
            if n < EVIN:
                return cols(a["ada_w"][0], n)
            if n < EVOUT:
                return cols(a["ev_w_in"][0], n - EVIN)
            if n < MOE0:
                return cols(a["ev_w_out"][0], n - EVOUT)
            if n < HYIN:
                return cols(a["ada_w"][1], n - ADA1)
            if n < HYOUT:
                return cols(a["hy_w_in"][0], n - HYIN)
            return cols(a["hy_w_out"][0], n - HYOUT)

        def used(n):
            if n < EVIN:
                return ada_mm, n + 1
            if n < EVOUT:
                return proj_mm, NT * (n - EVIN + 1)
            if n < MOE0:
                return mix_mm[0], NT * (n - EVOUT + 1)
            if n < HYIN:
                return ada_mm, 12 + n - ADA1 + 1
            if n < HYOUT:
                return hy_mm, 4 * (n - HYIN + 1)
            return mix_mm[1], NT * (n - HYOUT + 1)

        def full(n):
            return ring_full[n % RING], 16 * (n // RING + 1)

        def slot8(n):
            return ring[:, n % RING, :].rearrange("p (k n) -> p k n", k=KT)

        def slot4(n):
            return ring[:, n % RING, :].rearrange("p (k n) -> p k n", k=FT)

        def expert_weights(sp, layer, e, s):
            for j, name in enumerate(("moe_w_gate", "moe_w_up", "moe_w_down")):
                src = a[name][layer].rearrange("e d f -> (e d) f")
                rows = D if j < 2 else 512
                src = src[bass.ds(e * rows, rows), :].rearrange("(k p) n -> p k n", p=P)
                dst = slot8(s + j) if j < 2 else slot4(s + j)
                sp.dma_start(dst, src).then_inc(ring_full[(s + j) % RING], 16)

        block = ctx.enter_context(nc.Block())

        def counter(eng, name, value):
            reg = eng.alloc_register(name)
            eng.reg_mov(reg, value)
            return reg

        def wait_counted(eng, semaphore, reg, step):
            eng.wait_ge(semaphore, reg)
            eng.reg_add(reg, reg, step)

        def ln_rows(pool, n):
            off = LN_AT[n][0]
            l, s = n // 2, n % 2
            g = at(off, 2, D)
            pool.wait_ge(gate_out, 16 * 4 * (l + 1))
            for group in range(2):
                pool.dma_start(g[:, group, :], gates[l, s, group:group + 1, :].to_broadcast([P, D])).then_inc(lnrow_in, 16)
            pool.dma_start(at(off + 2 * D, D), a["ln_w"][l, s:s + 1, :].to_broadcast([P, D])).then_inc(lnrow_in, 16)
            pool.dma_start(at(off + 3 * D, D), a["ln_b"][l, s:s + 1, :].to_broadcast([P, D])).then_inc(lnrow_in, 16)

        def ln_sum(n, t):
            r = LN_AT[n][1]
            return picked[:, t, 0, :] if r is None else at(r + t * D, D)

        def pool_ln(pool, n):
            b = at(LN_AT[n][0] + 3 * D, D)
            pool.wait_ge(ln_w, NT * n + 1)
            pool.tensor_tensor(x[:, 0, :], ln_sum(n, 0), b, ALU.add).then_inc(x_rdy, 1)

        def pool_gates(pool, l):
            pool.wait_ge(mod_row, 12 * (l + 1))
            for s in range(2):
                for group in range(2):
                    c = 2 * D + 3 * D * s
                    pool.dma_start(gates[l, s, group:group + 1, :], mod_rows[l][group:group + 1, c:c + D]).then_inc(gate_out, 16)

        def pool_moe(pool, l):
            S = MS[l]
            pool.wait_ge(idx_rdy, 2 * (l + 1))
            pool.wait_ge(htok_act, 6 * (l + 1))
            if l == 0:
                pool.wait_ge(zeroed, 16 * ZERO_DMAS)
            for r in range(2):
                for t in range(NT):
                    pool.indirect_dma_start(slots[:, :], bass.IndirectOffsetOnAxis(ap=idx[:, r * NT + t:r * NT + t + 1], axis=0),
                                            h_tok[:, t, :], None).then_inc(scattered, 16)
            pool.wait_ge(scattered, 16 * 6 * (l + 1))
            pool.wait_ge(table_rdy, l + 1)
            blocks = pool.value_load(table[0:1, NE:NE + 1], min_val=NE, max_val=MAX_BLOCKS)
            pool.dma_start(slot_in, slots[BLK:2 * BLK, :]).then_inc(S["row_in"], 16)
            with pool.Fori(1, blocks + 1) as b:
                pool.wait_ge(S["rowT_mm"], b)
                pool.dma_start(slot_in, slots[bass.ds(b * BLK + BLK, BLK), :]).then_inc(S["row_in"], 16)
            pool.wait_ge(S["row_in"], blocks * 16 + 16)
            pool.wait_ge(S["slot_stored"], blocks * 16 + 32)
            pool.wait_ge(S["rowT"], blocks + 1)
            pool.tensor_tensor(idle, wsel[:, 0, 0:1], wsel[:, 0, 0:1], ALU.add).then_inc(idle_set, 1)
            pool.wait_ge(idle_set, l + 1)
            for t in range(NT):
                for r in range(2):
                    pool.indirect_dma_start(picked[:, t, r, :], None, slots[:, :],
                                            bass.IndirectOffsetOnAxis(ap=idx[:, r * NT + t:r * NT + t + 1], axis=0)).then_inc(gathered[t], 16)

        def hy_half_loads(pool, half):
            for k in range(2):
                pool.dma_start(w3[half][:, k, :], a["hy_ffn_w3"][0][:, k * D + half * 512:k * D + half * 512 + 512]).then_inc(taps_in[half], 16)
            pool.dma_start(win[half], a["c_win"][:, half * 512:half * 512 + 512].rearrange("(t p) n -> p t n", p=P)).then_inc(taps_in[half], 16)

        ROPED = (QR, KR, QD, KD)

        def act_proj_count(c):
            return sum(1 if k in ROPED else NT for k in range(c + 1))

        def dve_proj_count(c):
            return sum(2 if k in ROPED else 0 for k in range(c + 1))

        SCALAR_CHUNKS = 8

        def bias_by_matmul(l, c):
            return l == 1 and c < SCALAR_CHUNKS

        def act_ada(act, c):
            act.wait_ge(ada_mm, 12 + c + 1)
            act.activation(mod_rows[1][:, c * 512:(c + 1) * 512], bank[c % 2][0:2, :], ACT.Copy).then_inc(mod_row, 1)

        def pe_ada(pe, l):
            if l == 0:
                pe.wait_ge(cond_act, 1)
                pe.transpose(bank[7][:, 0:16], cond_rows, ident[0:16, 0:16]).then_inc(condT_mm, 1)
                pe.wait_ge(condT_rdy, 1)
            cT = condT.rearrange("p (g k) -> p k g", g=2)
            for c in range(12):
                n = (ADA0, ADA1)[l] + c
                pe.wait_ge(*full(n))
                if c >= 2:
                    pe.wait_ge(mod_row, 12 * l + c - 1)
                for k in range(KT):
                    last = pe.matmul(bank[c % 2][0:2, :], cT[:, k, :], slot8(n)[:, k, :], start=k == 0,
                                     stop=k == KT - 1 and not bias_by_matmul(l, c))
                if bias_by_matmul(l, c):
                    pe.wait_ge(adab_in, 16)
                    last = pe.matmul(bank[c % 2][0:2, :], ident[0:2, 0:2], ada_bias[:, c * 512:(c + 1) * 512], start=False, stop=True)
                last.then_inc(ada_mm, 1)
                if c >= 1:
                    pe_mod_columns(pe, l, c - 1)
            pe_mod_columns(pe, l, 11)

        def pe_mod_columns(pe, l, c):
            if c in (4, 5, 10, 11):
                return
            pe.wait_ge(mod_row, 12 * l + c + 1)
            for j in range(4):
                i = 4 * c + j
                last = pe.transpose(bank[2][:, 2 * i:2 * i + 2], mod_rows[l][:, i * P:(i + 1) * P], ident[0:2, 0:2])
            last.then_inc(modT_mm, 1)

        def pe_modulate(pe, m):
            for k in range(KT):
                if k >= 4:
                    pe.wait_ge(hT_dve if k % 2 else hT_act, 4 * m + (k - 4) // 2 + 1)
                for t in range(NT):
                    if k == 0 and m > 0:
                        pe.wait_ge(x_rdy, NT * (m - 1) + t + 1)
                    last = pe.transpose(bank[3 + k % 4][:, t * P:(t + 1) * P], x[:, t, k * P:(k + 1) * P], ident)
                last.then_inc(xT_mm, 1)

        def pe_projections(pe):
            pe.wait_ge(hT_act, 4)
            pe.wait_ge(hT_dve, 4)
            for c in range(EV_CHUNKS):
                n = EVIN + c
                pe.wait_ge(*full(n))
                if c >= 2:
                    pe.wait_ge(proj_act, act_proj_count(c - 2))
                    pe.wait_ge(proj_dve, dve_proj_count(c - 2))
                for t in range(NT):
                    for k in range(KT):
                        last = pe.matmul(bank[3 * (c % 2) + t], hT[:, k, t * P:(t + 1) * P], slot8(n)[:, k, :],
                                         start=k == 0, stop=k == KT - 1)
                    last.then_inc(proj_mm, 1)

        QKT = [(QR, qrT), (KR, krT), (QD, qdT), (KD, kdT)]

        def pe_mixer(pe):
            pe.wait_ge(proj_act, act_proj_count(6))
            pe.wait_ge(proj_dve, dve_proj_count(6))
            for u in range(16):
                c, _ = QKT[u // 4]
                if u >= 8:
                    pe.wait_ge(*((qkT_act if u % 2 == 0 else qkT_dve), (u - 8) // 2 + 1))
                for t in range(NT):
                    last = pe.transpose(bank[u % 8][:, t * P:(t + 1) * P], proj[:, t, c, (u % 4) * P:(u % 4 + 1) * P], ident)
                last.then_inc(qkT_mm, 1)
            pe.wait_ge(ck_in, 16)
            pe.wait_ge(qkT_act, 5)
            for h in range(H):
                last = pe.transpose(bank[0][:, h * P:(h + 1) * P], ck_raw[:, h * P:(h + 1) * P], ident)
            last.then_inc(qkT_mm, 1)
            pe.wait_ge(qkT_act, 9)
            pe.wait_ge(qkT_dve, 8)
            for t in range(NT):
                for h in range(H):
                    last = pe.matmul(bank[t][:, h * P:(h + 1) * P], krT[:, h, t * P:(t + 1) * P], qrT[:, h, t * P:(t + 1) * P],
                                     start=True, stop=True)
                last.then_inc(rsc_mm, 1)
            for s, (kz, t) in enumerate(KZ):
                pe.wait_ge(kz_dve, s + 1)
                for h in range(H):
                    last = pe.matmul(bank[3 + s][:, h * P:(h + 1) * P], kz[:, h * P:(h + 1) * P], proj[:, t, VR, h * P:(h + 1) * P],
                                     start=True, stop=True)
                last.then_inc(kv_mm, 1)
            pe.wait_ge(rsc_dve, 5)
            pe.wait_ge(kv_dve, 2)
            pe.wait_ge(mix_in, 16 * MIX_DMAS)
            for t in range(NT):
                b = bank[(7, 0, 1)[t]]
                for h in range(H):
                    o = b[:, h * P:(h + 1) * P]
                    pe_last = t == 0
                    last = pe.matmul(o, proj[:, t, QD, h * P:(h + 1) * P], proj[:, t, VR, h * P:(h + 1) * P], start=True, stop=pe_last)
                    if t:
                        fwd, bwd = (s0[:, 0], s1[:, 1]) if t == 1 else (s1[:, 0], s0[:, 1])
                        pe.matmul(o, qxi[:, 2 * (t - 1), h, :], fwd[:, h, :], start=False, stop=False)
                        last = pe.matmul(o, qxi[:, 2 * (t - 1) + 1, h, :], bwd[:, h, :], start=False, stop=True)
                last.then_inc(ret_mm, 1)
            pe.wait_ge(ret_dve, 3)
            pe.wait_ge(kv_act, 2)

            def scores(u):
                t, h = divmod(u, H)
                if u >= 2:
                    pe.wait_ge(dexp, u - 1)
                for r in range(2):
                    q = qdT[64 * r:64 * r + 64, h, t * P:(t + 1) * P]
                    b = bank[2 * (u % 2) + r]
                    if t == 0:
                        last = pe.matmul(b[:, 0:P], q, kdT[64 * r:64 * r + 64, h, 0:P], start=True, stop=True)
                    else:
                        pe.matmul(b[:, 0:2 * P], q, kdT[64 * r:64 * r + 64, h, P:T], start=True, stop=True)
                        last = pe.matmul(b[:, 2 * P:3 * P], q, ckT[64 * r:64 * r + 64, h, :], start=True, stop=True)
                last.then_inc(dsc_mm, 1)

            def to_keys(u):
                t = u // H
                pe.wait_ge(dcomb, u + 1)
                if u >= 1:
                    pe.wait_ge(daT, u)
                for j in range(1 if t == 0 else 3):
                    last = pe.transpose(bank[4][:, j * P:(j + 1) * P], adiff[:, u % 2, j * P:(j + 1) * P], ident)
                last.then_inc(daT_mm, 1)

            def values(u):
                t, h = divmod(u, H)
                pe.wait_ge(daT, u + 1)
                vs = [proj[:, 0, VD]] if t == 0 else [proj[:, 1, VD], proj[:, 2, VD], cv.rearrange("p h e -> p (h e)")]
                for j, v in enumerate(vs):
                    last = pe.matmul(bank[5 + t][:, h * P:(h + 1) * P], adT[:, u % 2, j * P:(j + 1) * P], v[:, h * P:(h + 1) * P],
                                     start=j == 0, stop=j == len(vs) - 1)
                last.then_inc(dpv_mm, 1)

            scores(0)
            for u in range(12):
                if u < 11:
                    scores(u + 1)
                to_keys(u)
                if u:
                    values(u - 1)
            values(11)
            pe.wait_ge(att_dve, 3)
            for k in range(KT):
                for t in range(NT):
                    src = proj[:, t, QR if k < 4 else QD, (k % 4) * P:(k % 4 + 1) * P]
                    last = pe.transpose(bank[k][:, t * P:(t + 1) * P], src, ident)
                last.then_inc(cT_mm, 1)
            pe.wait_ge(cT_act, 4)
            pe.wait_ge(cT_dve, 4)
            pe_output(pe, EVOUT, hT, mix_mm[0])

        def pe_output(pe, n0, src, done):
            for half in range(2):
                pe.wait_ge(*full(n0 + half))
                for t in range(NT):
                    for k in range(KT):
                        last = pe.matmul(bank[2 * t + half], src[:, k, t * P:(t + 1) * P], slot8(n0 + half)[:, k, :],
                                         start=k == 0, stop=k == KT - 1)
                    last.then_inc(done, 1)

        def pe_moe(pe, l, first):
            S = MS[l]
            m = 2 * l + 1
            pe.wait_ge(hT_act, 4 * (m + 1))
            pe.wait_ge(hT_dve, 4 * (m + 1))
            pe.wait_ge(router_in, 32)
            for t in range(NT):
                for k in range(KT):
                    last = pe.matmul(bank[7][:, t * NE:(t + 1) * NE], hT[:, k, t * P:(t + 1) * P], router_w[:, k, :],
                                     start=k == 0, stop=k == KT - 1)
            last.then_inc(rlog_mm, 1)
            for u in range(6):
                t, half = divmod(u, 2)
                for j in range(4):
                    last = pe.transpose(bank[u][:, j * P:(j + 1) * P], hT[:, 4 * half + j, t * P:(t + 1) * P], ident)
                last.then_inc(htok_mm, 1)
            pe.wait_ge(mask_rdy, l + 1)
            for t in range(NT):
                for s in range(t + 1):
                    pe.matmul(bank[6][:, t * NE:(t + 1) * NE], tri if s == t else ones, mask[:, s, :], start=s == 0, stop=s == t)
            for s in range(NT):
                last = pe.matmul(bank[6][:, NT * NE:(NT + 1) * NE], ones, mask[:, s, :], start=s == 0, stop=s == NT - 1)
            last.then_inc(pos_mm, 1)
            pe.wait_ge(htok_act, 6 * (l + 1))
            pe.wait_ge(table_rdy, l + 1)

            def rows_to_channels():
                wait_counted(pe, S["row_in"], rows_due, 16)
                for k in range(KT):
                    last = pe.transpose(bank[0 if k < 4 else 7][:, k % 4 * BLK:(k % 4 + 1) * BLK], slot_in[:, k * P:(k + 1) * P],
                                        ident[0:BLK, 0:BLK])
                last.then_inc(S["rowT_mm"], 1)

            def block_of_expert(b, s):
                pe.wait_ge(S["rowT"], b + 1)
                for w, bk, done in ((slot8(s), bank[1], "gate_mm"), (slot8(s + 1), bank[2], "up_mm")):
                    for f in range(FT):
                        for k in range(KT):
                            last = pe.matmul(bk[:, f * BLK:(f + 1) * BLK], w[:, k, f * P:(f + 1) * P], slot_inT[:, k, :],
                                             start=k == 0, stop=k == KT - 1)
                    last.then_inc(S[done], 1)
                rows_to_channels()
                results_to_rows()
                pe.wait_ge(S["act"], b + 1)
                w = slot4(s + 2)
                for half in range(2):
                    for j in range(4):
                        d = 4 * half + j
                        for f in range(FT):
                            last = pe.matmul(bank[3 + half][:, j * BLK:(j + 1) * BLK], w[:, f, d * P:(d + 1) * P], act_T[:, f, :],
                                             start=f == 0, stop=f == FT - 1)
                    last.then_inc(S["down_mm"], 1)

            def results_to_rows():
                wait_counted(pe, S["downT"], halves_due, 2)
                for k in range(KT):
                    last = pe.transpose(bank[5 + k // 4][0:BLK, k % 4 * P:(k % 4 + 1) * P], yT[:, k, :], ident)
                last.then_inc(S["back_mm"], 1)

            rows_due = counter(pe, f"rows_due{l}", 16)
            halves_due = counter(pe, f"halves_due{l}", 2)
            weights_due = [counter(pe, f"weights_due{l}{j}", full(first + j)[1]) for j in range(6)]
            rows_to_channels()
            with pe.Fori(0, NE // 2) as pair:
                edges = [pe.value_load(table[0:1, bass.ds(pair * 2 + j, 1)], min_val=0, max_val=MAX_BLOCKS) for j in range(3)]
                for e in range(2):
                    for j in range(3):
                        wait_counted(pe, full(first + 3 * e + j)[0], weights_due[3 * e + j], 16)
                    with pe.Fori(edges[e], edges[e + 1]) as b:
                        block_of_expert(b, first + 3 * e)
            results_to_rows()
            blocks = pe.value_load(table[0:1, NE:NE + 1], min_val=NE, max_val=MAX_BLOCKS)
            pe.wait_ge(S["rowT"], blocks + 1)
            pe.wait_ge(S["slot_evac"], blocks * 2 + 2)

        def pe_hyena(pe):
            pe.wait_ge(dft_in, 16 * 4)
            pe.matmul(bank[7][0:FH, 0:T], w1, feat, start=True, stop=True).then_inc(fmm, 1)
            pe.wait_ge(hT_act, 4 * 3)
            pe.wait_ge(hT_dve, 4 * 3)
            for c in range(HY_T):
                n = HYIN + c // 4
                pe.wait_ge(*full(n))
                if c >= 3:
                    pe.wait_ge(hy_dve, c - 2)
                if c == 3:
                    pe.wait_ge(fsin, 1)
                    pe.matmul(bank[7][0:FH, 0:T], w2, sinT, start=True, stop=True).then_inc(fmm, 1)
                for k in range(KT):
                    last = pe.matmul(bank[c % 3][:, 0:T], slot8(n)[:, k, (c % 4) * P:(c % 4 + 1) * P], hT[:, k, :],
                                     start=k == 0, stop=k == KT - 1)
                last.then_inc(hy_mm, 1)
            pe.wait_ge(hy_dve, HY_T)
            pe.wait_ge(fsin, 2)

            def taps(u):
                pe.wait_ge(taps_in[u // NT], 16 * 3)
                for semaphore, value in tap_banks_read[u]:
                    pe.wait_ge(semaphore, value)
                for r in range(2):
                    last = pe.matmul(bank[tap_bank(u) + r], sinT[:, u % NT * P:(u % NT + 1) * P], w3[u // NT][:, r, :],
                                     start=True, stop=True)
                last.then_inc(tap_mm, 1)

            tap_banks_read = [[], [], [(tap_dve, 1)], [(us_dve, 2)], [(us_dve, 3), (inv_dve, 4)], [(tap_dve, 4)]]

            def input_to_tokens(half):
                if half:
                    pe.wait_ge(ut_act, NT)
                for t in range(NT):
                    for j in range(4):
                        last = pe.transpose(bank[4 + t][:, j * P:(j + 1) * P], ufT[:, 4 * half + j, t * P:(t + 1) * P], ident)
                    last.then_inc(ut_mm, 1)

            taps(0)
            taps(1)
            input_to_tokens(0)
            taps(2)
            for half in range(2):
                if half:
                    taps(NT + 1)
                    taps(NT + 2)
                pe.wait_ge(tap_dve, NT * (half + 1))
                for m in range(NT):
                    u = NT * half + m
                    for comp in range(2):
                        if u >= 1:
                            pe.wait_ge(sp_act, 2 * (u - 1) + comp + 1)
                        pe_dft(pe, bank[2 + comp], hsd[:, comp], m, comp)
                        last_dft[0].then_inc(sp_mm, 1)
                pe.wait_ge(ut_act, NT * (half + 1))
                for m in range(NT):
                    u = NT * half + m
                    if m == 1:
                        pe.wait_ge(sp_act, 2 * NT * (half + 1))
                    if m == 2:
                        pe.wait_ge(us_dve, u - 1)
                    for comp in range(2):
                        pe_dft(pe, bank[us_bank(m) + comp], u_tok, m, comp)
                    last_dft[0].then_inc(us_mm, 1)
                if half == 0:
                    input_to_tokens(1)
                    taps(NT)
                pe.wait_ge(us_dve, NT * (half + 1))
                for j in range(4):
                    u = 4 * half + j
                    if u >= 2:
                        pe.wait_ge(inv_dve, u - 1)
                    b = bank[inv_bank(u)]
                    js = slice(j * P, (j + 1) * P)
                    pe.matmul(b[:, 0:P], spec[:, 0, 0, js], dft[:, 0:P], start=True, stop=False)
                    pe.matmul(b[:, 0:P], spec[:, 1, 0, js], dft[:, P:2 * P], start=False, stop=True)
                    for i in range(4):
                        comp, m = divmod(i, 2)
                        o = 256 + (comp * 2 + m) * 256
                        last = pe.matmul(b[:, P:T], spec[:, comp, 1 + m, js], dft[:, o:o + 256], start=i == 0, stop=i == 3)
                    last.then_inc(inv_mm, 1)
            pe.wait_ge(inv_dve, KT)
            pe_output(pe, HYOUT, x0T, mix_mm[1])

        def tap_bank(u):
            return 2 * (u % 2)

        def us_bank(m):
            return 2 * (m % 2)

        def inv_bank(u):
            return 0 if u % 2 else 7

        last_dft = [None]

        def pe_dft(pe, o, src, m, comp):
            if m == 0:
                last_dft[0] = pe.matmul(o, dft[:, comp * P:(comp + 1) * P], src[:, 0, :], start=True, stop=True)
                return
            for t in range(2):
                off = 256 + (comp * 2 + t) * 256 + (m - 1) * P
                last_dft[0] = pe.matmul(o, dft[:, off:off + P], src[:, 1 + t, :], start=t == 0, stop=t == 1)

        KZ = [(proj[:, 1, KD, :], 0), (proj[:, 2, KD, :], 0), (kz23[:, 0, :], 1), (kz23[:, 1, :], 2)]
        MIX_DMAS = 3
        ZERO_STEP = 6
        ZERO_DMAS = (MAX_BLOCKS + 2) // ZERO_STEP
        CONST_ALL = 16 * 6

        def chain(eng, s, count):
            def link(ins):
                count[0] += 1
                ins.then_inc(s, 1)
                eng.wait_ge(s, count[0])
            return link

        def filter_sine(act, i):
            act.wait_ge(farg, i + 1)
            act.activation(sinT, arg, ACT.Sin).then_inc(fsin, 1)

        def hy_dst(c):
            return x0T[:, c, :] if c < 8 else ufT[:, c - 8, :] if c < 16 else vT[:, c % 2, :]

        def mod_cols(m):
            sh = 24 * (m % 2)
            return (lambda k, g: modT[:, sh + 8 + k, g:g + 1]), (lambda k, g: modT[:, sh + k, g:g + 1])

        def act_modulate(act, m):
            scale, shift = mod_cols(m)
            act.wait_ge(modT_rdy, m // 2 + 1)
            for k in range(0, KT, 2):
                act.wait_ge(xT_mm, KT * m + k + 1)
                for g, ts in enumerate((slice(0, P), slice(P, T))):
                    last = act.activation(hT[:, k, ts], bank[3 + k % 4][:, ts], ACT.Identity, bias=shift(k, g), scale=scale(k, g))
                last.then_inc(hT_act, 1)

        def dve_modulate(dve, m):
            scale, shift = mod_cols(m)
            for k in range(1, KT, 2):
                dve.wait_ge(xT_mm, KT * m + k + 1)
                for g, ts in enumerate((slice(0, P), slice(P, T))):
                    last = dve.tensor_scalar(hT[:, k, ts], bank[3 + k % 4][:, ts], scale(k, g), shift(k, g), ALU.mult, ALU.add)
                last.then_inc(hT_dve, 1)

        def act_ln(act, n):
            if n == 1:
                act_ada(act, 0)
                act_ada(act, 1)
            if n % 2:
                for t in range(NT):
                    act.wait_ge(gathered[t], 32 * (n // 2 + 1))
                    act.activation(ln_sum(n, t), ln_sum(n, t), ACT.Copy, scale=wsel[:, 0, t:t + 1]).then_inc(ln_first, 1)
            if n == 1:
                act_ada(act, 2)
            for t in range(NT):
                if n == 1 and t == 2:
                    act_ada(act, 3)
                act.wait_ge(ln_var, NT * n + t + 1)
                act.activation(sd[:, t:t + 1], mv[:, t, 1:2], ACT.Sqrt, bias=eps_col, scale=1.0).then_inc(ln_sd, 1)
            for t in range(NT):
                act.wait_ge(ln_rstd, NT * n + t + 1)
                act.activation(ln_sum(n, t), ln_sum(n, t), ACT.Identity, bias=nmr[:, t:t + 1], scale=rstd[:, t:t + 1]).then_inc(ln_nrm, 1)
            if n == 1:
                for c in range(4, SCALAR_CHUNKS):
                    act_ada(act, c)

        def dve_ln(dve, link, n):
            off = LN_AT[n][0]
            g, w, b = at(off, 2, D), at(off + 2 * D, D), at(off + 3 * D, D)

            def total(t):
                r = ln_sum(n, t)
                gt = g[:, 0 if t == 0 else 1, :]
                if n % 2 == 0:
                    done = mix_mm[n // 2]
                    dve.wait_ge(done, NT + t + 1)
                    for half in range(2):
                        hs = slice(half * 512, half * 512 + 512)
                        last = dve.tensor_tensor(r[:, hs], bank[2 * t + half], gt[:, hs], ALU.mult)
                    last.then_inc(ln_in, 1)
                else:
                    dve.wait_ge(gathered[t], 32 * (n // 2 + 1))
                    dve.wait_ge(ln_first, NT * (n // 2) + t + 1)
                    link(dve.scalar_tensor_tensor(r, picked[:, t, 1, :], wsel[:, 1, t:t + 1], r, ALU.mult, ALU.add))
                    dve.tensor_tensor(r, r, gt, ALU.mult).then_inc(ln_in, 1)
                dve.wait_ge(ln_in, NT * n + t + 1)
                link(dve.scalar_tensor_tensor(r, x[:, t, :], ALPHA, r, ALU.mult, ALU.add))
                dve.bn_stats(stats[:, t, 0:6], r[:, 0:512])
                link(dve.bn_stats(stats[:, t, 6:12], r[:, 512:1024]))
                dve.bn_aggr(mv[:, t, :], stats[:, t, :]).then_inc(ln_var, 1)

            def inverse(t):
                dve.wait_ge(ln_sd, NT * n + t + 1)
                link(dve.reciprocal(rstd[:, t:t + 1], sd[:, t:t + 1]))
                dve.tensor_scalar(nmr[:, t:t + 1], mv[:, t, 0:1], rstd[:, t:t + 1], -1.0, ALU.mult, ALU.mult).then_inc(ln_rstd, 1)

            def weigh(t):
                dve.wait_ge(ln_nrm, NT * n + t + 1)
                dve.tensor_tensor(ln_sum(n, t), ln_sum(n, t), w, ALU.mult).then_inc(ln_w, 1)
                if t:
                    dve.wait_ge(ln_w, NT * n + t + 1)
                    dve.wait_ge(x_rdy, NT * n + t)
                    dve.tensor_tensor(x[:, t, :], ln_sum(n, t), b, ALU.add).then_inc(x_rdy, 1)

            dve.wait_ge(lnrow_in, 64 * (n + 1))
            if n == 0:
                dve.wait_ge(x_again, 32)
            total(0)
            total(1)
            inverse(0)
            total(2)
            inverse(1)
            weigh(0)
            inverse(2)
            weigh(1)
            weigh(2)

        def act_moe(act, l):
            S = MS[l]
            act.wait_ge(rlog_mm, l + 1)
            act.activation(score.rearrange("p t e -> p (t e)"), bank[7][:, 0:NT * NE], ACT.Sigmoid).then_inc(rscore, 1)
            for u in range(6):
                act.wait_ge(htok_mm, 6 * l + u + 1)
                act.activation(h_tok[:, u // 2, (u % 2) * 512:(u % 2) * 512 + 512], bank[u], ACT.Copy).then_inc(htok_act, 1)
            act.wait_ge(table_rdy, l + 1)
            act.sem_inc(S["slot_stored"], 16)
            blocks = act.value_load(table[0:1, NE:NE + 1], min_val=NE, max_val=MAX_BLOCKS)

            def store_before(b):
                act.wait_ge(S["slot_stored"], b * 16 + 16)
                act.wait_ge(S["back_mm"], b + 1)
                for half in range(2):
                    act.activation(slot_out[:, half * 512:half * 512 + 512], bank[5 + half][0:BLK, :], ACT.Copy).then_inc(S["slot_evac"], 1)
                act.wait_ge(S["slot_evac"], b * 2 + 2)
                act.dma_start(slots[bass.ds(b * BLK, BLK), :], slot_out).then_inc(S["slot_stored"], 16)

            with act.Fori(0, blocks) as b:
                act.wait_ge(S["gate_mm"], b + 1)
                act.activation(silu_g, bank[1][:, 0:FT * BLK], ACT.Silu).then_inc(S["silu"], 1)
                store_before(b)
                for half in range(2):
                    act.wait_ge(S["down_mm"], b * 2 + half + 1)
                    act.activation(yT[:, 4 * half:4 * half + 4, :].rearrange("p k s -> p (k s)"), bank[3 + half][:, 0:4 * BLK],
                                   ACT.Copy).then_inc(S["downT"], 1)
            if l == 0:
                act.wait_ge(S["rowT"], blocks + 1)
                act.dma_start(ada_bias, a["ada_b"][1:2, :].to_broadcast([2, 6 * D])).then_inc(adab_in, 16)
            store_before(blocks)

        def dve_moe(dve, link, l):
            S = MS[l]
            dve.wait_ge(rscore, l + 1)
            dve.wait_ge(router_in, 32)
            link(dve.tensor_tensor(sel, score, router_b.rearrange("p (o e) -> p o e", o=1).to_broadcast([P, NT, NE]), ALU.add))
            s4 = sel.rearrange("p t (g q) -> p (t g) q", q=4)
            dve.tensor_tensor(hi2, s4[:, :, 0:4:2], s4[:, :, 1:4:2], ALU.max)
            link(dve.tensor_tensor(lo2, s4[:, :, 0:4:2], s4[:, :, 1:4:2], ALU.min))
            dve.tensor_tensor(m1, hi2[:, :, 0], hi2[:, :, 1], ALU.max)
            dve.tensor_tensor(m2, hi2[:, :, 0], hi2[:, :, 1], ALU.min)
            link(dve.tensor_tensor(gs, lo2[:, :, 0], lo2[:, :, 1], ALU.max))
            link(dve.tensor_tensor(m2, m2, gs, ALU.max))
            link(dve.tensor_tensor(gs, m1, m2, ALU.add))

            def first_max(o, src, key, n):
                link(dve.tensor_reduce(rmx, src, AX, ALU.max))
                mb = rmx.rearrange("p (t o) -> p t o", o=1).to_broadcast([P, NT, n])
                link(dve.tensor_tensor(o, src, mb, ALU.is_equal))
                link(dve.tensor_tensor(o, o, key.rearrange("p (o e) -> p o e", o=1).to_broadcast([P, NT, n]), ALU.mult))
                link(dve.tensor_reduce(rmx, o, AX, ALU.max))
                link(dve.tensor_tensor(o, o, mb, ALU.is_equal))

            g3 = gs.rearrange("p (t g) -> p t g", g=NG)
            p3 = pen.rearrange("p (t g) -> p t g", g=NG)
            first_max(p3, g3, keep[:, K_KEYG:K_KEYG + NG], NG)
            link(dve.tensor_scalar(pen, pen, -1.0, BIG, ALU.add, ALU.mult))
            link(dve.tensor_tensor(selm.rearrange("p t (g q) -> p (t g) q", q=4), s4,
                                   pen.rearrange("p (g o) -> p g o", o=1).to_broadcast([P, NT * NG, 4]), ALU.add))
            key = keep[:, K_KEYE:K_KEYE + NE]
            first_max(oh0, selm, key, NE)
            link(dve.scalar_tensor_tensor(selm, oh0, -BIG, selm, ALU.mult, ALU.add))
            first_max(oh1, selm, key, NE)
            dve.tensor_tensor(mask, oh0, oh1, ALU.add).then_inc(mask_rdy, 1)
            for r, oh in enumerate((oh0, oh1)):
                link(dve.tensor_tensor(eq, oh, score, ALU.mult))
                link(dve.tensor_reduce(wsel[:, r, :], eq, AX, ALU.add))
            link(dve.tensor_tensor(wsel[:, 2, :], wsel[:, 0, :], wsel[:, 1, :], ALU.add))
            link(dve.reciprocal(wsel[:, 2, :], wsel[:, 2, :]))
            for r in range(2):
                link(dve.tensor_tensor(wsel[:, r, :], wsel[:, r, :], wsel[:, 2, :], ALU.mult))
            dve.wait_ge(pos_mm, l + 1)
            tot = bank[6][:, NT * NE:(NT + 1) * NE]
            link(dve.tensor_scalar(nblk[:, 0, :], tot, float(BLK), 1.0, ALU.is_gt, ALU.add))
            for m in range(2, T // BLK):
                link(dve.scalar_tensor_tensor(nblk[:, 0, :], tot, float(m * BLK), nblk[:, 0, :], ALU.is_gt, ALU.add))
            cur, nxt = 0, 1
            for step in (1, 2, 4, 8):
                dve.tensor_copy(nblk[:, nxt, 0:step], nblk[:, cur, 0:step])
                link(dve.tensor_tensor(nblk[:, nxt, step:NE], nblk[:, cur, step:NE], nblk[:, cur, 0:NE - step], ALU.add))
                cur, nxt = nxt, cur
            dve.memset(base[:, 0:1], 0.0)
            link(dve.tensor_copy(base[:, 1:NE + 1], nblk[:, cur, :]))
            dve.tensor_copy(table[0:1, :], base[0:1, :]).then_inc(table_rdy, 1)
            b3 = base[:, 0:NE].rearrange("p (o e) -> p o e", o=1).to_broadcast([P, NT, NE])
            pos = bank[6][:, 0:NT * NE].rearrange("p (t e) -> p t e", e=NE)
            link(dve.scalar_tensor_tensor(soff, b3, float(BLK), pos, ALU.mult, ALU.add))
            for r, oh in enumerate((oh0, oh1)):
                link(dve.tensor_tensor(eq, oh, soff, ALU.mult))
                link(dve.tensor_reduce(slot_f[:, r, :], eq, AX, ALU.add))
                dve.tensor_scalar(idx[:, r * NT:(r + 1) * NT], slot_f[:, r, :], float(BLK), None, ALU.add).then_inc(idx_rdy, 1)
            dve.wait_ge(table_rdy, l + 1)
            blocks = dve.value_load(table[0:1, NE:NE + 1], min_val=NE, max_val=MAX_BLOCKS)
            dve.memset(yT, 0.0).then_inc(S["downT"], 2)
            flat = slot_inT.rearrange("p k s -> p (k s)")
            half = 4 * BLK
            dve.wait_ge(S["rowT_mm"], 1)
            dve.tensor_copy(flat[:, 0:half], bank[0][:, 0:half])
            dve.tensor_copy(flat[:, half:], bank[7][:, 0:half]).then_inc(S["rowT"], 1)
            with dve.Fori(0, blocks) as b:
                dve.wait_ge(S["up_mm"], b + 1)
                dve.wait_ge(S["silu"], b + 1)
                dve.tensor_tensor(act_T.rearrange("p f s -> p (f s)"), silu_g, bank[2][:, 0:FT * BLK], ALU.mult).then_inc(S["act"], 1)
                dve.wait_ge(S["rowT_mm"], b + 2)
                dve.tensor_copy(flat[:, 0:half], bank[0][:, 0:half])
                dve.tensor_copy(flat[:, half:], bank[7][:, 0:half]).then_inc(S["rowT"], 1)

        def dve_ada(dve, link, l):
            dve.wait_ge(first_in, 16 * 4)
            if l == 1:
                dve.wait_ge(adab_in, 16)
                dve.wait_ge(mod_row, 12 + SCALAR_CHUNKS)
            for c in range(12):
                if bias_by_matmul(l, c):
                    continue
                dve.wait_ge(ada_mm, 12 * l + c + 1)
                cs = slice(c * 512, c * 512 + 512)
                dve.tensor_tensor(mod_rows[l][:, cs], bank[c % 2][0:2, :], ada_bias[:, cs], ALU.add).then_inc(mod_row, 1)
            dve.wait_ge(modT_mm, 8 * (l + 1))
            cols2 = bank[2][:, 0:96].rearrange("p (c g) -> p c g", g=2)
            for s in range(2):
                dve.tensor_copy(modT[:, 24 * s:24 * s + 8, :], cols2[:, 24 * s:24 * s + 8, :])
                last = dve.tensor_scalar(modT[:, 24 * s + 8:24 * s + 16, :], cols2[:, 24 * s + 8:24 * s + 16, :], 1.0, None, ALU.add)
            last.then_inc(modT_rdy, 1)
            dve.wait_ge(modT_rdy, l + 1)

        @block.sync
        def _(sp):
            for dst, src in ((cond_rows[0:8, :], a["c_ctx"].rearrange("(k p) -> k p", p=P)),
                             (cond_rows[8:16, :], a["c"][0].rearrange("(k p) -> k p", p=P)), (keep[:, :], a["c_keep"])):
                sp.dma_start(dst, src).then_inc(first_in, 16)
            sp.dma_start(ada_bias, a["ada_b"][0:1, :].to_broadcast([2, 6 * D])).then_inc(first_in, 16)

            def load(n):
                if n >= RING:
                    before = n - RING
                    if MOE0 <= before < ADA1:
                        expert_through(0, (before - MOE0) // 3)
                    else:
                        sp.wait_ge(*used(before))
                sp.dma_start(slot8(n), chunk_src(n)).then_inc(ring_full[n % RING], 16)

            def expert_through(layer, e):
                ends = sp.value_load(table[0:1, bass.ds(e + 1, 1)], min_val=1, max_val=MAX_BLOCKS)
                sp.wait_ge(MS[layer]["down_mm"], ends * 2)

            def load_moe(layer, first):
                for e in range(2):
                    for j in range(3):
                        sp.wait_ge(*used(first + 3 * e + j - RING))
                    expert_weights(sp, layer, e, first + 3 * e)
                sp.wait_ge(table_rdy, layer + 1)
                with sp.Fori(1, NE // 2) as pair:
                    for e in range(2):
                        expert_through(layer, pair * 2 + (e - 2))
                        expert_weights(sp, layer, pair * 2 + e, first + 3 * e)

            for n in range(MOE0):
                load(n)
            load_moe(0, MOE0)
            for n in range(ADA1, MOE1):
                load(n)
            load_moe(1, MOE1)
            for t in range(NT):
                sp.wait_ge(x_rdy, 3 * NT + t + 1)
                sp.dma_start(out[0][0] if t == 0 else out[1][0, (t - 1) * P:t * P, :], x[:, t, :]).then_inc(x_out, 16)
            sp.wait_ge(x_out, 16 * NT)
            sp.wait_ge(out_done, 16 * OUT_DMAS)

        @block.gpsimd
        def gpsimd_program(pool):
            pool.dma_start(mixc, a["c_mix"]).then_inc(mixc_in, 16)
            pool.dma_start(router_w, a["router_w"].rearrange("(k p) e -> p k e", p=P)).then_inc(router_in, 16)
            pool.dma_start(router_b, a["router_bias"].rearrange("(o e) -> o e", o=1).to_broadcast([P, NE])).then_inc(router_in, 16)
            pool.dma_start(s0[:, 0], a["state_ret_fwd"][0, 0].rearrange("h d e -> d h e")).then_inc(mix_in, 16)
            pool.dma_start(s0[:, 1], a["state_ret_bwd"][0, 0].rearrange("h d e -> d h e")).then_inc(mix_in, 16)
            pool.dma_start(cv, a["cache_diff_v"][0, 0]).then_inc(mix_in, 16)
            pool_gates(pool, 0)
            pool.wait_ge(hyc_mm, 1)
            pool.memset(zeros, 0.0).then_inc(zero_rdy, 1)
            pool.wait_ge(zero_rdy, 1)
            rows = slots.rearrange("(b r) n -> r b n", r=BLK)
            for b in range(0, MAX_BLOCKS + 2, ZERO_STEP):
                pool.dma_start(rows[:, b:b + ZERO_STEP, :],
                               zeros.rearrange("p (o n) -> p o n", o=1).to_broadcast([BLK, ZERO_STEP, D])).then_inc(zeroed, 16)
            pool.wait_ge(xT_mm, KT)
            pool.dma_start(ck_raw, a["cache_diff_k"][0, 0].rearrange("t h d -> t (h d)")).then_inc(ck_in, 16)
            pool.wait_ge(proj_act, act_proj_count(KD))
            pool.dma_start(out[2][0, 0].rearrange("t h d -> t (h d)"), proj[:, 0, KD, :]).then_inc(out_done, 16)
            pool.wait_ge(proj_act, act_proj_count(VD))
            pool.dma_start(out[3][0, 0].rearrange("t h d -> t (h d)"), proj[:, 0, VD, :]).then_inc(out_done, 16)
            pool.wait_ge(kv_act, 2)
            for k in range(2):
                pool.dma_start(out[4 + k][0, 0].rearrange("h d e -> d h e"), s_out[:, k]).then_inc(out_done, 16)
            pool.wait_ge(daT, 12)
            pool.wait_ge(dpv_mm, 12)
            pool.dma_start(x[:, 0, :], a["x_prompt"][0]).then_inc(x_again, 16)
            pool.dma_start(x[:, 1:3, :], a["x_sample"][0].rearrange("(t p) d -> p t d", p=P)).then_inc(x_again, 16)
            pool.wait_ge(cT_mm, KT)
            pool.wait_ge(out_done, 16 * 4)
            ln_rows(pool, 0)
            pool_ln(pool, 0)
            ln_rows(pool, 1)
            pool_moe(pool, 0)
            pool_ln(pool, 1)
            pool.wait_ge(x_rdy, 2 * NT)
            pool.dma_start(dft, a["c_dft"]).then_inc(dft_in, 16)
            pool.dma_start(feat, a["c_feat"]).then_inc(dft_in, 16)
            pool_gates(pool, 1)
            pool.wait_ge(gate_out, 16 * 8)
            pool.dma_start(w1, a["hy_ffn_w1"][0]).then_inc(dft_in, 16)
            pool.dma_start(w2, a["hy_ffn_w2"][0]).then_inc(dft_in, 16)
            hy_half_loads(pool, 0)
            pool.wait_ge(hy_mm, HY_T)
            hy_half_loads(pool, 1)
            pool.wait_ge(inv_mm, KT)
            ln_rows(pool, 2)
            pool_ln(pool, 2)
            pool.wait_ge(x_rdy, 9)
            ln_rows(pool, 3)
            pool_moe(pool, 1)
            pool_ln(pool, 3)

        @block.tensor
        def tensor_program(pe):
            pe.wait_ge(first_in, 16 * 4)
            pe_ada(pe, 0)
            pe.wait_ge(hy_in_s, 16 * 5)
            pe.transpose(bank[7][:, 128:232], hy_rows, ident[0:104, 0:104]).then_inc(hyc_mm, 1)
            pe.wait_ge(x_in, 32)
            pe_modulate(pe, 0)
            pe_projections(pe)
            pe_mixer(pe)
            pe.wait_ge(ln_in, NT)
            pe_modulate(pe, 1)
            pe_moe(pe, 0, MOE0)
            pe_ada(pe, 1)
            pe_modulate(pe, 2)
            pe_hyena(pe)
            pe.wait_ge(ln_in, 3 * NT)
            pe_modulate(pe, 3)
            pe_moe(pe, 1, MOE1)

        @block.scalar
        def scalar_program(act):
            link = chain(act, act_chain, [0])
            one_dma = [
                (decay[:, 0:H], a["ret_decay_fwd"].to_broadcast([P, H])),
                (decay[:, H:2 * H], a["ret_decay_bwd"].to_broadcast([P, H])),
                (lam_in.rearrange("p a b -> p (a b)"), a["diff_lambda"].rearrange("o a b -> o (a b)").to_broadcast([P, 256])),
                (subln, a["diff_subln_w"].to_broadcast([P, P])),
                (gn_w, a["ret_gn_w"].to_broadcast([P, 512])),
            ]
            act.wait_ge(first_in, 16 * 4)
            act.activation(cond_rows, cond_rows, ACT.Silu).then_inc(cond_act, 1)
            act.dma_start(x[:, 0, :], a["x_prompt"][0]).then_inc(x_in, 16)
            act.dma_start(x[:, 1:3, :], a["x_sample"][0].rearrange("(t p) d -> p t d", p=P)).then_inc(x_in, 16)
            for dst, src in one_dma:
                act.dma_start(dst, src).then_inc(const_in, 16)
            act.dma_start(hy_rows[0:72, :], a["hy_conv_w"][0].rearrange("w (c p) -> (w c) p", p=P)).then_inc(hy_in_s, 16)
            act.dma_start(hy_rows[72:96, :], a["hy_conv_b"][0].rearrange("(c p) -> c p", p=P)).then_inc(hy_in_s, 16)
            act.dma_start(hy_rows[96:104, :], a["hy_filter_bias"][0].rearrange("(c p) -> c p", p=P)).then_inc(hy_in_s, 16)
            for j, name in enumerate(("hy_freq", "hy_ffn_b1", "hy_ffn_b2")):
                act.dma_start(ffn_cols[:, j:j + 1], a[name][0].rearrange("(p o) -> p o", o=1)).then_inc(const_in if j == 0 else hy_in_s, 16)
            act_modulate(act, 0)
            act.wait_ge(const_in, CONST_ALL)

            act.activation(lgt[:, 0, :], decay, ACT.Exp, scale=math.log(2.0)).then_inc(tab_act, 1)
            act.wait_ge(tab_dve, 1)
            act.activation(lgt[:, 2, :], lgt[:, 1, :], ACT.Ln).then_inc(tab_act, 1)
            act.wait_ge(lg_rdy, 1)
            act.wait_ge(mixc_in, 16)
            for h in range(H):
                act.activation(decay_T[:, h, :], mixc[:, M_RELF:M_RELF + P], ACT.Exp, scale=lg[:, h:h + 1])
                act.activation(decay_bwd[:, h, :], mixc[:, M_RELB:M_RELB + P], ACT.Exp, scale=lg[:, H + h:H + h + 1])
                act.activation(xi_f[:, h, :], mixc[:, M_XI:M_XI + P], ACT.Exp, scale=lg[:, h:h + 1])
                act.activation(xi_b[:, h, :], mixc[:, M_XB:M_XB + P], ACT.Exp, scale=lg[:, H + h:H + h + 1])
            act.activation(zeta[:, 0, :], lg[:, 0:H], ACT.Exp, scale=keep[:, K_LEFT:K_LEFT + 1])
            act.activation(zeta[:, 1, :], lg[:, H:2 * H], ACT.Exp, scale=keep[:, K_J:K_J + 1])
            act.activation(lam[:, 2:4], lam[:, 0:2], ACT.Exp)
            act.activation(g_chunk, lg, ACT.Exp, scale=float(P)).then_inc(tab_act, 1)

            act.wait_ge(gate_out, 16 * 4)
            for c in range(EV_CHUNKS):
                for t in range(1 if c in ROPED else NT):
                    act.wait_ge(proj_mm, NT * c + t + 1)
                    act.activation(proj[:, t, c, :], bank[3 * (c % 2) + t], ACT.Silu if c == GR else ACT.Copy).then_inc(proj_act, 1)
            for u in range(0, 17, 2):
                act.wait_ge(qkT_mm, u + 1)
                if u < 16:
                    act.activation(QKT[u // 4][1][:, u % 4, :], bank[u % 8][:, 0:T], ACT.Copy).then_inc(qkT_act, 1)
                else:
                    act.activation(ckT.rearrange("p h t -> p (h t)"), bank[0], ACT.Copy).then_inc(qkT_act, 1)
            for s in range(2):
                act.wait_ge(kv_mm, s + 1)
                act.wait_ge(zeroed, 16 * ZERO_DMAS)
                act.activation(s_out[:, s].rearrange("p h e -> p (h e)"), bank[3 + s], ACT.Copy).then_inc(kv_act, 1)
            for t in range(NT):
                act.wait_ge(ret_var, t + 1)
                act.activation(hsd_[:, t, :], hmv[:, t, :, 1], ACT.Sqrt, bias=eps_col, scale=1.0).then_inc(ret_sd, 1)

            def exps(u):
                t = u // H
                n = P if t == 0 else 3 * P
                act.wait_ge(dmax, u + 1)
                if u >= 2:
                    act.wait_ge(dcomb, u - 1)
                for r in range(2):
                    last = act.activation(probs[:, u % 2, r, 0:n], bank[2 * (u % 2) + r][:, 0:n], ACT.Exp,
                                          bias=nmx[:, u, r:r + 1], scale=QK_SCALE, accum_out=ssum[:, u, r:r + 1])
                last.then_inc(dexp, 1)

            act.wait_ge(ret_mm, 3)
            exps(0)
            for u in range(12):
                if u < 11:
                    exps(u + 1)
                act.wait_ge(daT_mm, u + 1)
                if u >= 2:
                    act.wait_ge(dpv_mm, u - 1)
                n = P if u < H else 3 * P
                act.activation(adT[:, u % 2, 0:n], bank[4][:, 0:n], ACT.Copy).then_inc(daT, 1)
            for t in range(NT):
                act.wait_ge(att_ss, t + 1)
                act.activation(hsd_[:, t, :], hmv[:, t, :, 0], ACT.Sqrt, bias=eps_col, scale=1.0 / P).then_inc(att_sd, 1)
            for k in range(0, KT, 2):
                act.wait_ge(cT_mm, k + 1)
                act.activation(hT[:, k, :], bank[k][:, 0:T], ACT.Copy).then_inc(cT_act, 1)
            act_ln(act, 0)
            act_modulate(act, 1)
            act_moe(act, 0)
            act_ln(act, 1)
            act_modulate(act, 2)
            filter_sine(act, 0)
            for c in range(HY_T):
                if c == 3:
                    filter_sine(act, 1)
                act.wait_ge(hy_mm, c + 1)
                if c == 0:
                    act.wait_ge(hyc, 1)
                if c >= 18:
                    act.wait_ge(hy_dve, c - 1)
                act.activation(hy_dst(c), bank[c % 3][:, 0:T], ACT.Identity, bias=hy_cols[:, 72 + c:73 + c],
                               scale=hy_cols[:, 24 + c:25 + c]).then_inc(hy_act, 1)
            for half in range(2):
                for t in range(NT):
                    act.wait_ge(ut_mm, NT * half + t + 1)
                    act.activation(u_tok[:, t, :], bank[4 + t], ACT.Copy).then_inc(ut_act, 1)
                for m in range(NT):
                    for comp in range(2):
                        act.wait_ge(sp_mm, 2 * (NT * half + m) + comp + 1)
                        act.activation(spec[:, comp, m, :], bank[2 + comp], ACT.Copy, scale=keep[:, K_WF + m:K_WF + m + 1]).then_inc(sp_act, 1)
            act_ln(act, 2)
            act_modulate(act, 3)
            act_moe(act, 1)
            act_ln(act, 3)

        @block.vector
        def vector_program(dve):
            link = chain(dve, dve_chain, [0])
            dve.memset(eps_col, EPS)
            dve.wait_ge(condT_mm, 1)
            dve.tensor_copy(condT, bank[7][:, 0:16]).then_inc(condT_rdy, 1)
            dve_ada(dve, link, 0)
            dve.wait_ge(hyc_mm, 1)
            dve.tensor_copy(hy_cols, bank[7][:, 128:232]).then_inc(hyc, 1)
            dve_modulate(dve, 0)
            dve.wait_ge(const_in, CONST_ALL)
            dve.wait_ge(tab_act, 1)
            dve.tensor_scalar(lgt[:, 1, :], lgt[:, 0, :], -1.0, 1.0, ALU.mult, ALU.add).then_inc(tab_dve, 1)
            dve.wait_ge(tab_dve, 1)
            link(dve.tensor_scalar(lgt[:, 3, :], lgt[:, 1, :], -1.0, 1.0, ALU.mult, ALU.add))
            is0 = lg
            link(dve.tensor_scalar(is0, lgt[:, 3, :], 0.0, None, ALU.is_equal))
            link(dve.tensor_tensor(lgt[:, 3, :], lgt[:, 3, :], is0, ALU.add))
            link(dve.reciprocal(lgt[:, 3, :], lgt[:, 3, :]))
            link(dve.tensor_tensor(lgt[:, 3, :], lgt[:, 3, :], lgt[:, 0, :], ALU.mult))
            link(dve.tensor_tensor(is0, is0, lgt[:, 0, :], ALU.mult))
            dve.wait_ge(tab_act, 2)
            link(dve.tensor_tensor(lgt[:, 3, :], lgt[:, 3, :], lgt[:, 2, :], ALU.mult))
            dve.wait_ge(xT_mm, KT)
            lm = at(0, 2, 64, src=xf)
            link(dve.tensor_tensor(lm, lam_in[:, 0:4:2, :], lam_in[:, 1:4:2, :], ALU.mult))
            link(dve.tensor_reduce(lam[:, 0:2], lm, AX, ALU.add))
            link(dve.tensor_scalar(subln, subln, 1.0 - LAM_INIT, None, ALU.mult))
            dve.tensor_tensor(lg, lgt[:, 3, :], is0, ALU.subtract).then_inc(lg_rdy, 1)
            dve.wait_ge(tab_act, 3)
            link(dve.scalar_tensor_tensor(lam[:, 0:1], lam[:, 3:4], -LAM_INIT, lam[:, 2:3], ALU.add, ALU.subtract))
            link(dve.tensor_scalar(zeta, zeta, P ** -0.5, None, ALU.mult))
            for h in range(H):
                dve.tensor_tensor(decay_T[:, h, :], decay_T[:, h, :], mixc[:, M_MF:M_MF + P], ALU.mult)
                link(dve.tensor_tensor(decay_bwd[:, h, :], decay_bwd[:, h, :], mixc[:, M_MB:M_MB + P], ALU.mult))
            link(dve.tensor_tensor(decay_T, decay_T, decay_bwd, ALU.add))

            dve.wait_ge(gate_out, 16 * 4)
            for c in ROPED:
                heads, cc, ss, w = (H, M_RC, M_RS, 128) if c in (QR, KR) else (2 * H, M_DC, M_DS, 64)
                q = w // 4
                for t in (1, 2):
                    dve.wait_ge(proj_mm, NT * c + t + 1)
                    src, dst = bank[3 * (c % 2) + t], proj[:, t, c, :]
                    cos = mixc[:, cc + (t - 1) * w:cc + t * w].rearrange("p (o n) -> p o n", o=1).to_broadcast([P, heads, w])
                    dve.tensor_tensor(rope_tmp.rearrange("p (h n) -> p h n", n=w), src.rearrange("p (h n) -> p h n", n=w), cos, ALU.mult)
                    s5 = src.rearrange("p (h a two q) -> p h a two q", a=2, two=2, q=q)
                    d5 = dst.rearrange("p (h a two q) -> p h a two q", a=2, two=2, q=q)
                    sin = mixc[:, ss + (t - 1) * w:ss + t * w].rearrange("p (o a two q) -> p o a two q", o=1, a=2, two=2)
                    for two in range(2):
                        last = dve.tensor_tensor(d5[:, :, :, two, :], s5[:, :, :, 1 - two, :],
                                                 sin[:, :, :, two, :].to_broadcast([P, heads, 2, q]), ALU.mult)
                    link(last)
                    dve.tensor_tensor(dst, dst, rope_tmp, ALU.add).then_inc(proj_dve, 1)
                    dve.wait_ge(proj_dve, dve_proj_count(c) - 2 + t)
            for u in range(1, 16, 2):
                dve.wait_ge(qkT_mm, u + 1)
                dve.tensor_copy(QKT[u // 4][1][:, u % 4, :], bank[u % 8][:, 0:T]).then_inc(qkT_dve, 1)

            dve.wait_ge(qkT_mm, 17)
            for s, (kz, t) in enumerate(KZ):
                dve.tensor_tensor(kz.rearrange("p (h d) -> p h d", h=H), proj[:, t, KR, :].rearrange("p (h d) -> p h d", h=H),
                                  zeta[:, s % 2, :].rearrange("p (h o) -> p h o", o=1).to_broadcast([P, H, P]), ALU.mult).then_inc(kz_dve, 1)
            dve.wait_ge(qkT_act, 8)
            for t in (1, 2):
                for k, xi in enumerate((xi_f, xi_b)):
                    last = dve.tensor_tensor(qxi[:, 2 * (t - 1) + k], qrT[:, :, t * P:(t + 1) * P], xi, ALU.mult)
                last.then_inc(rsc_dve, 1)
            for t in range(NT):
                dve.wait_ge(rsc_mm, t + 1)
                dve.tensor_tensor(proj[:, t, QD, :], bank[t], decay_T.rearrange("p h i -> p (h i)"), ALU.mult).then_inc(rsc_dve, 1)
            dve.wait_ge(mix_in, 16 * MIX_DMAS)
            for k in range(2):
                dve.wait_ge(kv_mm, 3 + k)
                for h in range(H):
                    last = dve.scalar_tensor_tensor(s1[:, k, h, :], s0[:, k, h, :], g_chunk[:, H * k + h:H * k + h + 1],
                                                    bank[5 + k][:, h * P:(h + 1) * P], ALU.mult, ALU.add)
                last.then_inc(kv_dve, 1)
            for t in range(NT):
                b = bank[(7, 0, 1)[t]]
                dve.wait_ge(ret_mm, t + 1)
                for h in range(H):
                    last = dve.bn_stats(hstat[:, h, :], b[:, h * P:(h + 1) * P])
                link(last)
                for h in range(H):
                    last = dve.bn_aggr(hmv[:, t, h, :], hstat[:, h, :])
                last.then_inc(ret_var, 1)
                dve.wait_ge(ret_sd, t + 1)
                link(dve.reciprocal(hrs[:, t, :], hsd_[:, t, :]))
                for h in range(H):
                    last = dve.tensor_scalar(proj[:, t, QR, h * P:(h + 1) * P], b[:, h * P:(h + 1) * P], hmv[:, t, h, 0:1],
                                             hrs[:, t, h:h + 1], ALU.subtract, ALU.mult)
                link(last)
                link(dve.tensor_tensor(proj[:, t, QR, :], proj[:, t, QR, :], gn_w, ALU.mult))
                dve.tensor_tensor(proj[:, t, QR, :], proj[:, t, QR, :], proj[:, t, GR, :], ALU.mult).then_inc(ret_dve, 1)

            def row_max(u):
                n = P if u < H else 3 * P
                dve.wait_ge(dsc_mm, u + 1)
                for r in range(2):
                    last = dve.tensor_reduce(mx[:, u, r:r + 1], bank[2 * (u % 2) + r][:, 0:n], AX, ALU.max)
                link(last)
                dve.tensor_scalar(nmx[:, u, :], mx[:, u, :], -QK_SCALE, None, ALU.mult).then_inc(dmax, 1)

            def combine(u):
                n = P if u < H else 3 * P
                dve.wait_ge(dexp, u + 1)
                link(dve.reciprocal(rsum[:, u, :], ssum[:, u, :]))
                link(dve.tensor_scalar(rsum[:, u, 1:2], rsum[:, u, 1:2], lam[:, 0:1], None, ALU.mult))
                if u >= 2:
                    dve.wait_ge(daT_mm, u - 1)
                link(dve.tensor_scalar(adiff[:, u % 2, 0:n], probs[:, u % 2, 1, 0:n], rsum[:, u, 1:2], None, ALU.mult))
                dve.scalar_tensor_tensor(adiff[:, u % 2, 0:n], probs[:, u % 2, 0, 0:n], rsum[:, u, 0:1], adiff[:, u % 2, 0:n],
                                         ALU.mult, ALU.add).then_inc(dcomb, 1)

            row_max(0)
            for u in range(12):
                if u < 11:
                    row_max(u + 1)
                combine(u)
            dve.wait_ge(ret_dve, 3)
            for t in range(NT):
                dve.wait_ge(dpv_mm, H * (t + 1))
                o = proj[:, t, QD, :]
                link(dve.tensor_copy(o, bank[5 + t]))
                sq = qdT.rearrange("p h t -> p (h t)")[:, 0:512]
                if t == 0:
                    dve.wait_ge(dsc_mm, 12)
                link(dve.tensor_tensor(sq, o, o, ALU.mult))
                dve.tensor_reduce(hmv[:, t, :, 0], sq.rearrange("p (h e) -> p h e", h=H), AX, ALU.add).then_inc(att_ss, 1)
                dve.wait_ge(att_ss, t + 1)
            for t in range(NT):
                dve.wait_ge(att_sd, t + 1)
                link(dve.reciprocal(hrs[:, t, :], hsd_[:, t, :]))
                for h in range(H):
                    hs = slice(h * P, (h + 1) * P)
                    last = dve.scalar_tensor_tensor(proj[:, t, QD, hs], bank[5 + t][:, hs], hrs[:, t, h:h + 1], subln, ALU.mult, ALU.mult)
                last.then_inc(att_dve, 1)
            for k in range(1, KT, 2):
                dve.wait_ge(cT_mm, k + 1)
                dve.tensor_copy(hT[:, k, :], bank[k][:, 0:T]).then_inc(cT_dve, 1)
            dve_ln(dve, link, 0)
            dve_modulate(dve, 1)
            dve_moe(dve, link, 0)
            dve_ln(dve, link, 1)
            dve_ada(dve, link, 1)

            dve_modulate(dve, 2)
            dve.wait_ge(hy_in_s, 16 * 5)

            def filter_argument(i):
                dve.wait_ge(fmm, i + 1)
                if i:
                    dve.wait_ge(fsin, 1)
                link(dve.tensor_scalar(arg, bank[7][0:FH, 0:T], ffn_cols[:, 1 + i:2 + i], ffn_cols[:, 0:1], ALU.add, ALU.mult))
                link(dve.tensor_scalar(turns, arg, 1 / (2 * math.pi), ROUND, ALU.mult, ALU.add))
                link(dve.tensor_scalar(turns, turns, ROUND, None, ALU.subtract))
                link(dve.scalar_tensor_tensor(arg, turns, -TWO_PI_HI, arg, ALU.mult, ALU.add))
                link(dve.scalar_tensor_tensor(arg, turns, -TWO_PI_LO, arg, ALU.mult, ALU.add))
                dve.tensor_scalar(arg, arg, 3.1415925, -3.1415925, ALU.min, ALU.max).then_inc(farg, 1)

            filter_argument(0)
            for c in range(HY_T):
                if c == 3:
                    filter_argument(1)
                dve.wait_ge(hy_act, c + 1)
                d, s = hy_dst(c), bank[c % 3]
                w0, w2_ = hy_cols[:, c:c + 1], hy_cols[:, 48 + c:49 + c]
                dve.scalar_tensor_tensor(d[:, 1:CTX], s[:, 0:CTX - 1], w0, d[:, 1:CTX], ALU.mult, ALU.add)
                link(dve.scalar_tensor_tensor(d[:, CTX + 1:T], s[:, CTX:T - 1], w0, d[:, CTX + 1:T], ALU.mult, ALU.add))
                dve.scalar_tensor_tensor(d[:, 0:CTX - 1], s[:, 1:CTX], w2_, d[:, 0:CTX - 1], ALU.mult, ALU.add)
                last = dve.scalar_tensor_tensor(d[:, CTX:T - 1], s[:, CTX + 1:T], w2_, d[:, CTX:T - 1], ALU.mult, ALU.add)
                if c >= 16:
                    link(last)
                    last = dve.tensor_tensor(ufT[:, c - 16, :], ufT[:, c - 16, :], d, ALU.mult)
                last.then_inc(hy_dve, 1)

            def window_taps(u):
                half, t = divmod(u, NT)
                dve.wait_ge(taps_in[half], 16 * 3)
                dve.wait_ge(tap_mm, u + 1)
                if u == NT:
                    dve.wait_ge(sp_mm, 2 * NT)
                f, b, tmp = hsd[:, 0, t, :], hsd[:, 1, t, :], prod[:, 2 + t % 2, :]
                dve.tensor_tensor(tmp, bank[tap_bank(u)], win[half][:, t, :], ALU.mult)
                link(dve.tensor_tensor(b, bank[tap_bank(u) + 1], win[half][:, t, :], ALU.mult))
                if t < 2:
                    link(dve.memset(b[0:1, :], 0.0))
                link(dve.tensor_tensor(f, tmp, b, ALU.add))
                dve.tensor_tensor(b, tmp, b, ALU.subtract).then_inc(tap_dve, 1)

            for u in range(NT):
                window_taps(u)
            for half in range(2):
                if half:
                    window_taps(NT + 1)
                    window_taps(NT + 2)
                for m in range(NT):
                    u = NT * half + m
                    dve.wait_ge(us_mm, u + 1)
                    ur, us = bank[us_bank(m)], bank[us_bank(m) + 1]
                    hr, hs = spec[:, 0, m, :], spec[:, 1, m, :]
                    if m == 0:
                        dve.wait_ge(sp_act, 2 * NT * (half + 1))
                    dve.tensor_tensor(prod[:, 0, :], ur, hr, ALU.mult)
                    dve.tensor_tensor(prod[:, 1, :], us, hs, ALU.mult)
                    dve.tensor_tensor(prod[:, 2, :], ur, hs, ALU.mult)
                    link(dve.tensor_tensor(prod[:, 3, :], us, hr, ALU.mult))
                    dve.tensor_tensor(hr, prod[:, 0, :], prod[:, 1, :], ALU.subtract)
                    dve.tensor_tensor(hs, prod[:, 2, :], prod[:, 3, :], ALU.add).then_inc(us_dve, 1)
                    dve.wait_ge(us_dve, u + 1)
                if half == 0:
                    window_taps(NT)
                for j in range(4):
                    k = 4 * half + j
                    dve.wait_ge(inv_mm, k + 1)
                    link(dve.scalar_tensor_tensor(ufT[:, k, :], ufT[:, k, :], hy_cols[:, 96 + k:97 + k], bank[inv_bank(k)][:, 0:T],
                                                  ALU.mult, ALU.add))
                    dve.tensor_tensor(x0T[:, k, :], x0T[:, k, :], ufT[:, k, :], ALU.mult).then_inc(inv_dve, 1)
            dve_ln(dve, link, 2)
            dve_modulate(dve, 3)
            dve_moe(dve, link, 1)
            dve_ln(dve, link, 3)


_INS = ['x_prompt', 'x_sample', 'cache_diff_k', 'cache_diff_v', 'state_ret_fwd', 'state_ret_bwd', 'c', 'c_ctx',
        'ada_w', 'ada_b', 'ln_w', 'ln_b', 'ev_w_in', 'ev_w_out', 'ret_decay_fwd', 'ret_decay_bwd', 'ret_gn_w',
        'diff_lambda', 'diff_subln_w', 'hy_w_in', 'hy_conv_w', 'hy_conv_b', 'hy_ffn_w1', 'hy_ffn_b1', 'hy_ffn_w2',
        'hy_ffn_b2', 'hy_ffn_w3', 'hy_freq', 'hy_filter_bias', 'hy_w_out', 'router_w', 'router_bias',
        'moe_w_gate', 'moe_w_up', 'moe_w_down']
_OUTS = [(1, 128, 1024), (1, 256, 1024), (1, 1, 128, 4, 128), (1, 1, 128, 4, 128), (1, 1, 4, 128, 128), (1, 1, 4, 128, 128)]


def kernel(**inputs):
    import concourse.bacc as _bacc
    from concourse.bass_utils import run_bass_kernel_spmd as _run

    nc = _bacc.Bacc("TRN2", target_bir_lowering=False, num_devices=1)
    arrays, args = {}, {}
    for name, value in [(n, inputs[n]) for n in _INS] + list(constants().items()):
        v = np.ascontiguousarray(value)
        arrays[f"in_{name}_dram"] = v
        args[name] = nc.dram_tensor(f"in_{name}_dram", v.shape, mybir.dt.from_np(v.dtype), kind="ExternalInput").ap()
    outs = [nc.dram_tensor(f"out_{i}_dram", shape, F32, kind="ExternalOutput").ap() for i, shape in enumerate(_OUTS)]
    trunk_program(nc, args, outs)
    r = _run(nc, [arrays], core_ids=[0])
    return tuple(r.results[0][f"out_{i}_dram"] for i in range(len(_OUTS)))
```
